# Optimizing a Trainium2 kernel written in Bass

```python
import jax, jax.numpy as jnp
from jax import lax
import numpy as np

D_MODEL = 1024
BATCH = 1
SEQ = 256
DEPTH = 1

GRID_W = 64
NA_HEADS = 8
NA_HEAD_DIM = 64
NA_ROWS = 8
NA_COLS = 16
SWA_Q_HEADS = 8
SWA_KV_HEADS = 2
SWA_HEAD_DIM = 64
SWA_WINDOW = 128
SWA_BLOCK = 128
ROPE_THETA = 10000.0
N_EXPERTS = 32
TOP_K = 4
D_FF_EXPERT = 1024
SWIGLU_LIMIT = 7.0
SWIGLU_ALPHA = 1.702
EXPERT_BLOCK = 256
RMS_EPS = 1e-5

NA_WIDTH = NA_HEADS * NA_HEAD_DIM
SWA_Q_WIDTH = SWA_Q_HEADS * SWA_HEAD_DIM
SWA_KV_WIDTH = SWA_KV_HEADS * SWA_HEAD_DIM
IN_SIZES = (NA_WIDTH, NA_WIDTH, NA_WIDTH, SWA_Q_WIDTH, SWA_KV_WIDTH, SWA_KV_WIDTH, D_MODEL, D_MODEL)
D_IN = sum(IN_SIZES)
IN_SPLITS = tuple(int(v) for v in np.cumsum(IN_SIZES)[:-1])

kernel_name = 'hybrid_natten_swa_moe_encoder'

def rmsnorm(x, g):
    xf = x.astype(jnp.float32)
    y = xf * lax.rsqrt(jnp.mean(xf * xf, axis=-1, keepdims=True) + RMS_EPS)
    return (y * g.astype(jnp.float32)).astype(x.dtype)

def rope(x, pos):
    half = x.shape[-1] // 2
    inv_freq = ROPE_THETA ** (-jnp.arange(half, dtype=jnp.float32) / half)
    ang = pos.astype(jnp.float32)[:, None] * inv_freq[None, :]
    cos = jnp.cos(ang)[None, :, None, :]
    sin = jnp.sin(ang)[None, :, None, :]
    xf = x.astype(jnp.float32)
    x1, x2 = xf[..., :half], xf[..., half:]
    return jnp.concatenate([x1 * cos - x2 * sin, x2 * cos + x1 * sin], axis=-1).astype(x.dtype)

def neighborhood_attention(q, k, v, rpb):
    b, s, h, dh = q.shape
    rows = s // GRID_W
    kr = min(NA_ROWS, rows)
    scale = dh ** -0.5
    qg = q.reshape(b, rows, GRID_W, h, dh)
    kg = k.reshape(b, rows, GRID_W, h, dh)
    vg = v.reshape(b, rows, GRID_W, h, dh)
    col = np.arange(GRID_W)
    cstart = np.clip(col - NA_COLS // 2, 0, GRID_W - NA_COLS)
    cidx = cstart[:, None] + np.arange(NA_COLS)[None, :]
    rpb_c = rpb[:, :, cidx - col[:, None] + NA_COLS - 1]

    def one_row(r):
        rs = jnp.clip(r - kr // 2, 0, rows - kr)
        kw = lax.dynamic_slice_in_dim(kg, rs, kr, axis=1)[:, :, cidx]
        vw = lax.dynamic_slice_in_dim(vg, rs, kr, axis=1)[:, :, cidx]
        qr = lax.dynamic_index_in_dim(qg, r, axis=1, keepdims=False)
        sc = jnp.einsum('bchd,bicjhd->bhcij', qr, kw).astype(jnp.float32) * scale
        dr = rs + jnp.arange(kr) - r + NA_ROWS - 1
        bias = jnp.take(rpb_c, dr, axis=1).transpose(0, 2, 1, 3)
        sc = sc + bias[None].astype(jnp.float32)
        p = jax.nn.softmax(sc.reshape(b, h, GRID_W, kr * NA_COLS), axis=-1)
        p = p.reshape(b, h, GRID_W, kr, NA_COLS).astype(v.dtype)
        return jnp.einsum('bhcij,bicjhd->bchd', p, vw)

    out = lax.map(one_row, jnp.arange(rows))
    return out.transpose(1, 0, 2, 3, 4).reshape(b, s, h * dh)

def sliding_window_gqa(q, k, v, sinks):
    b, s, hq, dh = q.shape
    hkv = k.shape[2]
    grp = hq // hkv
    nb = s // SWA_BLOCK
    scale = dh ** -0.5
    pad = ((0, 0), (SWA_BLOCK, SWA_BLOCK), (0, 0), (0, 0))
    kp = jnp.pad(k, pad).reshape(b, nb + 2, SWA_BLOCK, hkv, dh)
    vp = jnp.pad(v, pad).reshape(b, nb + 2, SWA_BLOCK, hkv, dh)
    kband = jnp.concatenate([kp[:, :-2], kp[:, 1:-1], kp[:, 2:]], axis=2)
    vband = jnp.concatenate([vp[:, :-2], vp[:, 1:-1], vp[:, 2:]], axis=2)
    qb = q.reshape(b, nb, SWA_BLOCK, hkv, grp, dh)
    sc = jnp.einsum('bnqkgd,bnjkd->bkgnqj', qb, kband).astype(jnp.float32) * scale
    qpos = jnp.arange(SWA_BLOCK)[:, None]
    koff = jnp.arange(3 * SWA_BLOCK)[None, :] - SWA_BLOCK
    rel_ok = jnp.abs(koff - qpos) <= SWA_WINDOW
    kabs = jnp.arange(nb)[:, None] * SWA_BLOCK + koff
    in_seq = (kabs >= 0) & (kabs < s)
    mask = rel_ok[None, :, :] & in_seq[:, None, :]
    sc = jnp.where(mask[None, None, None], sc, -jnp.inf)
    sink = sinks.astype(jnp.float32).reshape(1, hkv, grp, 1, 1, 1)
    m = jnp.maximum(jnp.max(sc, axis=-1, keepdims=True), sink)
    e = jnp.exp(sc - m)
    p = (e / (jnp.sum(e, axis=-1, keepdims=True) + jnp.exp(sink - m))).astype(v.dtype)
    o = jnp.einsum('bkgnqj,bnjkd->bnqkgd', p, vband)
    return o.reshape(b, s, hq * dh)

def moe_clamped_swiglu(h, w_router, b_router, w1, b1, w2, b2):
    b, s, d = h.shape
    t = b * s
    xt = h.reshape(t, d)
    logits = (xt @ w_router + b_router).astype(jnp.float32)
    top_v, top_i = lax.top_k(logits, TOP_K)
    gates = jax.nn.softmax(top_v, axis=-1)
    n_assign = t * TOP_K
    e_id = top_i.reshape(n_assign).astype(jnp.int32)
    tok = jnp.arange(n_assign, dtype=jnp.int32) // TOP_K
    wts = gates.reshape(n_assign)
    order = jnp.argsort(e_id, stable=True)
    e_sorted = e_id[order]
    counts = jnp.bincount(e_id, length=N_EXPERTS)
    start = jnp.cumsum(counts) - counts
    padded = (counts + EXPERT_BLOCK - 1) // EXPERT_BLOCK * EXPERT_BLOCK
    pend = jnp.cumsum(padded)
    pstart = pend - padded
    dest = pstart[e_sorted] + jnp.arange(n_assign, dtype=jnp.int32) - start[e_sorted]
    n_rows = n_assign + N_EXPERTS * EXPERT_BLOCK
    n_blk = n_rows // EXPERT_BLOCK
    row_tok = jnp.full((n_rows,), t, jnp.int32).at[dest].set(tok[order])
    row_w = jnp.zeros((n_rows,), jnp.float32).at[dest].set(wts[order])
    blk_exp = jnp.minimum(jnp.searchsorted(pend, jnp.arange(n_blk) * EXPERT_BLOCK, side='right'), N_EXPERTS - 1)
    x_ext = jnp.concatenate([xt, jnp.zeros((1, d), xt.dtype)], axis=0)

    def expert_block(args):
        rows, ex = args
        xb = x_ext[rows]
        gu = xb @ w1[ex] + b1[ex]
        gate = jnp.minimum(gu[:, :D_FF_EXPERT], SWIGLU_LIMIT)
        up = jnp.clip(gu[:, D_FF_EXPERT:], -SWIGLU_LIMIT, SWIGLU_LIMIT)
        glu = gate * jax.nn.sigmoid(gate * SWIGLU_ALPHA)
        return ((up + 1.0) * glu) @ w2[ex] + b2[ex]

    yb = lax.map(expert_block, (row_tok.reshape(n_blk, EXPERT_BLOCK), blk_exp))
    contrib = yb.reshape(n_rows, d).astype(jnp.float32) * row_w[:, None]
    y = jax.ops.segment_sum(contrib, row_tok, num_segments=t + 1)[:t]
    return y.reshape(b, s, d).astype(h.dtype)

def setup_inputs(seed: int = 0) -> dict:
    key = jax.random.key(seed)
    ks = jax.random.split(key, 18)
    f32 = jnp.float32

    def nrm(k, shape, scale):
        return jax.random.normal(k, shape, f32) * scale

    return {
        'x': nrm(ks[0], (BATCH, SEQ, D_MODEL), 1.0),
        'norm1_g': 1.0 + nrm(ks[1], (DEPTH, D_MODEL), 0.02),
        'w_in': nrm(ks[2], (DEPTH, D_MODEL, D_IN), D_MODEL ** -0.5),
        'b_in': nrm(ks[3], (DEPTH, D_IN), 0.02),
        'na_rpb': nrm(ks[4], (DEPTH, NA_HEADS, 2 * NA_ROWS - 1, 2 * NA_COLS - 1), 0.5),
        'swa_sinks': nrm(ks[5], (DEPTH, SWA_Q_HEADS), 1.0),
        'w_up_a': nrm(ks[6], (DEPTH, NA_WIDTH, D_MODEL), NA_WIDTH ** -0.5),
        'w_up_b': nrm(ks[7], (DEPTH, SWA_Q_WIDTH, D_MODEL), SWA_Q_WIDTH ** -0.5),
        'w_out': nrm(ks[8], (DEPTH, D_MODEL, D_MODEL), D_MODEL ** -0.5),
        'norm2_g': 1.0 + nrm(ks[9], (DEPTH, D_MODEL), 0.02),
        'w_router': nrm(ks[10], (DEPTH, D_MODEL, N_EXPERTS), D_MODEL ** -0.5),
        'b_router': nrm(ks[11], (DEPTH, N_EXPERTS), 0.01),
        'w1': nrm(ks[12], (DEPTH, N_EXPERTS, D_MODEL, 2 * D_FF_EXPERT), D_MODEL ** -0.5),
        'b1': nrm(ks[13], (DEPTH, N_EXPERTS, 2 * D_FF_EXPERT), 0.02),
        'w2': nrm(ks[14], (DEPTH, N_EXPERTS, D_FF_EXPERT, D_MODEL), D_FF_EXPERT ** -0.5),
        'b2': nrm(ks[15], (DEPTH, N_EXPERTS, D_MODEL), 0.02),
        'final_g': 1.0 + nrm(ks[16], (D_MODEL,), 0.02),
    }

def reference(x, norm1_g, w_in, b_in, na_rpb, swa_sinks, w_up_a, w_up_b, w_out,
              norm2_g, w_router, b_router, w1, b1, w2, b2, final_g):
    b, s, _ = x.shape
    pos = jnp.arange(s, dtype=jnp.int32)
    for l in range(DEPTH):
        h = rmsnorm(x, norm1_g[l])
        proj = h @ w_in[l] + b_in[l]
        qa, ka, va, qb, kb, vb, ga, gb = jnp.split(proj, IN_SPLITS, axis=-1)
        oa = neighborhood_attention(
            qa.reshape(b, s, NA_HEADS, NA_HEAD_DIM),
            ka.reshape(b, s, NA_HEADS, NA_HEAD_DIM),
            va.reshape(b, s, NA_HEADS, NA_HEAD_DIM),
            na_rpb[l])
        ob = sliding_window_gqa(
            rope(qb.reshape(b, s, SWA_Q_HEADS, SWA_HEAD_DIM), pos),
            rope(kb.reshape(b, s, SWA_KV_HEADS, SWA_HEAD_DIM), pos),
            vb.reshape(b, s, SWA_KV_HEADS, SWA_HEAD_DIM),
            swa_sinks[l])
        merged = jax.nn.sigmoid(ga) * (oa @ w_up_a[l]) + jax.nn.sigmoid(gb) * (ob @ w_up_b[l])
        x = x + merged @ w_out[l]
        h2 = rmsnorm(x, norm2_g[l])
        x = x + moe_clamped_swiglu(h2, w_router[l], b_router[l], w1[l], b1[l], w2[l], b2[l])
    return rmsnorm(x, final_g)


_drawn_inputs = setup_inputs


def setup_inputs(seed=0):
    import zlib

    import numpy as np

    out = dict(_drawn_inputs(seed))
    spreads = {}
    factors = {'swa_sinks': 64.0,
     'b1': 14.988,
     'b2': 17.365,
     'final_g': 23.39,
     'norm1_g': 3.84,
     'norm2_g': 4.646,
     'b_router': 5.13}
    for name, (base, spread) in spreads.items():
        noise = np.random.default_rng([zlib.crc32(name.encode()), seed]).standard_normal(out[name].shape)
        drawn = base * np.exp(spread * noise) if base else spread * noise
        out[name] = __import__('jax').numpy.asarray(drawn.astype(out[name].dtype))
    for name, factor in factors.items():
        out[name] = (out[name] * factor).astype(out[name].dtype)
    return out
```

```python
from contextlib import ExitStack

import numpy as np

import concourse.bass as bass
from concourse import mybir

F32 = mybir.dt.float32
I32 = mybir.dt.int32
ALU = mybir.AluOpType
ACT = mybir.ActivationFunctionType
AX = mybir.AxisListType

P = 128
D = 1024
T = 256
MT = T // P
KD = D // P
GRID_W, ROWS, NA_ROWS, NA_COLS = 64, 4, 8, 16
HEADS, DH = 8, 64
NA_W = HEADS * DH
KV_HEADS = 2
WINDOW = 128
THETA = 10000.0
E, TOPK, FF = 32, 4, 1024
LIMIT, ALPHA, EPS = 7.0, 1.702, 1e-5
D_IN = 3 * NA_W + NA_W + 2 * KV_HEADS * DH + 2 * D
SCALE = DH ** -0.5

CW = 256
SLOT_F = 2048
SLOTS = 12
N_IN = D_IN // CW
N_UP = 4
N_OUT = D // CW
PRE = N_IN + N_UP + N_OUT
W1_CH, W2_CH = D // P, FF // (2 * P)
CAP = 64
OVER = 16
OVER_MAX = T * TOPK // (CAP + 1)
NBC = E + OVER
DR = 6
RPB_W = 2 * NA_COLS - 1
RPB = (2 * NA_ROWS - 1) * RPB_W
NEG = -1.0e30
FAR = 4096.0

_W = [("ident", P), ("rot", P), ("dup", 2 * P), ("dup_rot", 2 * P), ("cos", T), ("sin", T),
      ("na_mask", GRID_W), ("swa_mask", MT * T), ("before", P), ("slot", P), ("over", OVER), ("expert", 1)]
CONST = {}
_at = 0
for _n, _w in _W:
    CONST[_n] = slice(_at, _at + _w)
    _at += _w
CONST_W = _at


def shape_constants():
    c = np.zeros((P, CONST_W), np.float32)
    half = DH // 2
    i = np.arange(P)
    c[:, CONST["ident"]] = np.eye(P)
    rot = np.zeros((P, P), np.float32)
    for d in range(P):
        if d % DH < half:
            rot[d + half, d] = -1.0
        else:
            rot[d - half, d] = 1.0
    c[:, CONST["rot"]] = rot
    for g in range(KV_HEADS):
        dup = np.zeros((P, P), np.float32)
        dup[g * DH + i % DH, i] = 1.0
        c[:, CONST["dup"]][:, g * P:(g + 1) * P] = dup
        c[:, CONST["dup_rot"]][:, g * P:(g + 1) * P] = rot @ dup
    inv = (THETA ** (-np.arange(half, dtype=np.float32) / half)).astype(np.float32)
    ang = np.arange(T, dtype=np.float32)[None, :] * inv[i % half][:, None]
    c[:, CONST["cos"]] = np.cos(ang)
    c[:, CONST["sin"]] = np.sin(ang)
    col = i % GRID_W
    first = np.clip(col - NA_COLS // 2, 0, GRID_W - NA_COLS)[:, None]
    key = np.arange(GRID_W)[None, :]
    near = np.where((key >= first) & (key < first + NA_COLS), 0.0, NEG)
    c[:, CONST["na_mask"]] = near.reshape(P // GRID_W, GRID_W, GRID_W)[:, ::-1].reshape(P, GRID_W)
    q = np.arange(MT)[None, :, None] * P + i[:, None, None]
    k = np.arange(T)[None, None, :]
    c[:, CONST["swa_mask"]] = np.where(np.abs(k - q) <= WINDOW, 0.0, NEG).reshape(P, MT * T)
    c[:, CONST["before"]] = i[:, None] < i[None, :]
    c[:, CONST["slot"]] = i[None, :] % CAP
    c[:, CONST["over"]] = np.arange(OVER)[None, :]
    c[:, CONST["expert"]] = i[:, None]
    return c


class Chain:

    def __init__(self, eng, sem):
        self.eng, self.sem, self.base, self.n = eng, sem, 0, 0

    def link(self, ins):
        ins.then_inc(self.sem, 1)
        self.n += 1
        self.eng.wait_ge(self.sem, self.base + self.n)


def build_block(nc, consts, x_in, norm1_g, w_in, b_in, na_rpb, swa_sinks, w_up_a, w_up_b, w_out,
                norm2_g, w_router, b_router, w1, b1, w2, b2, final_g, out):
    with ExitStack() as ctx:
        def sb(name, shape, dt=F32):
            return ctx.enter_context(nc.sbuf_tensor(name, shape, dt))

        def sem(name):
            return ctx.enter_context(nc.semaphore(name))

        ring = sb("ring", [P, SLOTS, SLOT_F])
        cst = sb("cst", [P, CONST_W])
        x = sb("x", [P, MT, D])
        hT = sb("hT", [P, KD, T])
        h2 = hT[:].rearrange("p k t -> p (k t)").rearrange("p (m d) -> p m d", m=MT)
        gates = sb("gates", [P, 2 * KD, T])
        h = gates[:, 0:KD, :].rearrange("p k t -> p (k t)").rearrange("p (m d) -> p m d", m=MT)
        merged = gates[:, 0:KD, :]
        h2T = gates[:, KD:2 * KD, :]
        work = sb("work", [P, 4736])
        cut = lambda a, n: work[:, a:a + n]
        qaT = cut(0, 1024).rearrange("p (b t) -> p b t", t=T)
        kaT = cut(1024, 1024).rearrange("p (b t) -> p b t", t=T)
        oT = cut(2048, 2048).rearrange("p (b t) -> p b t", t=T)
        kbT = cut(4096, 512).rearrange("p (g t) -> p g t", t=T)
        xg = cut(0, 512)
        xgT = cut(512, 512)
        gate_s, up_s, sig_s, hid = (cut(1024 + 512 * n, 512) for n in range(4))
        hidT = cut(3072, 512)
        down_s = cut(3584, 512)
        scatT = cut(4096, 256)
        pick = cut(4352, 128).rearrange("p (m s) -> p m s", m=MT)
        pick_g = cut(4480, 256).rearrange("p (m s) -> p m s", m=MT)
        qbT = sb("qbT", [P, 4, T])
        kraw = sb("kraw", [P, T])
        rtmp = sb("rtmp", [P, 2, T])
        rtmp2 = sb("rtmp2", [P, 2, T])
        v_sb = sb("v_sb", [P, MT, NA_W + P])
        v_bias = sb("v_bias", [P, NA_W + P])
        tables = sb("tables", [P, HEADS * DR * GRID_W])
        na_bias = tables[:].rearrange("p (h w) -> p h w", h=HEADS)
        b1_sb = tables[0:E, 0:2 * FF]
        b2_sb = tables[0:E, 2 * FF:2 * FF + D]
        prob = [sb(f"prob{n}", [P, 2, MT, T]) for n in range(2)]
        probT = sb("probT", [P, 2, 2, T])
        vec_rows = sb("vec_rows", [P, P])
        n_vec = D_IN // P + KD
        vec = sb("vec", [P, n_vec])
        g2_b = sb("g2_b", [P, D])
        gf_b = qbT[:].rearrange("p b t -> p (b t)")
        sink_b = sb("sink_b", [P, HEADS])
        wr = sb("wr", [P, KD, E])
        br = sb("br", [E, 1])
        ones = sb("ones", [P, P])
        zeros = sb("zeros", [1, 512])
        minus_half = sb("minus_half", [P, MT])
        ssq = sb("ssq", [P, 3, MT])
        msq = sb("msq", [P, 3, MT])
        rstd = sb("rstd", [P, 3, MT])
        mx = sb("mx", [P, 2, 2])
        neg_mx = sb("neg_mx", [P, 2, 2])
        den = sb("den", [P, 2, 2])
        e_sink = sb("e_sink", [P, 2, 2])
        logT = kraw[0:E, :]
        logit = sb("logit", [P, MT, E])
        top8 = sb("top8", [P, MT, 8])
        n_gt = sb("n_gt", [P, MT])
        neg_top = sb("neg_top", [P, MT])
        g_sum = sb("g_sum", [P, MT])
        above = sb("above", [P, MT, E])
        equal = sb("equal", [P, MT, E])
        nth = sb("nth", [P, MT, E])
        chosen = sb("chosen", [P, MT, E])
        place = sb("place", [P, MT, NBC])
        share = sb("share", [P, MT, NBC])
        is_exp = sb("is_exp", [E, NBC])
        shareT, placeT = rtmp[0:E, 0, :], rtmp[0:E, 1, :]
        extra = sb("extra", [E, 4])
        from_j = sb("from_j", [E, OVER])
        sel_off = sb("sel_off", [E, OVER])
        ctrl = sb("ctrl", [1, OVER + 1], I32)
        b1_pick = sb("b1_pick", [E, CAP])

        bank = ctx.enter_context(nc.psum_tensor("bank", [P, 8, 512], F32))
        quarter = lambda b: bank[:, b, :].rearrange("p (a t) -> p a t", t=P)
        half_ = lambda b: bank[:, b, :].rearrange("p (a t) -> p a t", t=T)

        x_landed, consts_landed, vec_landed = sem("x_landed"), sem("consts_landed"), sem("vec_landed")
        attn_small_landed, bias_landed = sem("attn_small_landed"), sem("bias_landed")
        final_g_landed = sem("final_g_landed")
        route_landed, expert_bias_landed = sem("route_landed"), sem("expert_bias_landed")
        landed = [sem(f"chunk_landed{n}") for n in range(SLOTS)]
        chunk_used = sem("chunk_used")
        dve_step = sem("dve_step")
        pool_step = sem("pool_step")
        ones_set, ssq_dve, ssq_act = sem("ones_set"), sem("ssq_dve"), sem("ssq_act")
        msq_ready, rstd_ready, h_ready = sem("msq_ready"), sem("rstd_ready"), sem("h_ready")
        hT_done, hT_ready = sem("hT_done"), sem("hT_ready")
        vec_done, vec_ready = sem("vec_done"), sem("vec_ready")
        proj_read_dve, proj_read_act = sem("proj_read_dve"), sem("proj_read_act")
        masked_bias, rope_done, rope_ready = sem("masked_bias"), sem("rope_done"), sem("rope_ready")
        scores_done, max_ready, exp_ready = sem("scores_done"), sem("max_ready"), sem("exp_ready")
        prob_ready, probT_done, probT_ready = sem("prob_ready"), sem("probT_done"), sem("probT_ready")
        o_done, o_ready, sig_ready = sem("o_done"), sem("o_ready"), sem("sig_ready")
        merged_ready, x2_ready = sem("merged_ready"), sem("x2_ready")
        h2_ready, h2T_done, h2T_ready = sem("h2_ready"), sem("h2T_done"), sem("h2T_ready")
        logT_done, logT_ready, log_done = sem("logT_done"), sem("logT_ready"), sem("log_done")
        top_ready, top_exp, chosen_ready, count_done = sem("top_ready"), sem("top_exp"), sem("chosen_ready"), sem("count_done")
        place_ready, extra_ready, start_done = sem("place_ready"), sem("extra_ready"), sem("start_done")
        tr_done, tr_ready, list_done, ctrl_ready = sem("tr_done"), sem("tr_ready"), sem("list_done"), sem("ctrl_ready")
        pick_ready, pick_g_ready, b1_pick_ready = sem("pick_ready"), sem("pick_g_ready"), sem("b1_pick_ready")
        xg_done, xg_ready, xgT_done, xgT_ready = sem("xg_done"), sem("xg_ready"), sem("xgT_done"), sem("xgT_ready")
        gate_ready, sigm_ready, hid_ready = sem("gate_ready"), sem("sigm_ready"), sem("hid_ready")
        hidT_done, hidT_ready = sem("hidT_done"), sem("hidT_ready")
        scatT_done, scatT_ready, down_ready, scatter_done = sem("scatT_done"), sem("scatT_ready"), sem("down_ready"), sem("scatter_done")
        y_done, out_ready, out_stored = sem("y_done"), sem("out_ready"), sem("out_stored")

        def C(name):
            return cst[:, CONST[name]]

        def slot_of(chunk):
            return chunk % SLOTS

        def landings(chunk):
            return 16 * (chunk // SLOTS + 1)

        def expert_slot(c):
            return slot_of(PRE + c), landings(PRE + c)

        BLK = W1_CH + W2_CH
        assert BLK == SLOTS and N_IN * CW == D_IN

        UNITS = HEADS
        FIRST_U = 6
        ROPE_U = 3
        GATE_C = 9
        BS, BT, BO, BK = 3, 5, 7, 2
        BG, BU, BX, BH = 4, 5, 6, 7

        def from_right(v):
            v = v.rearrange("p (r c) -> p r c", c=GRID_W)
            return bass.AP(v.tensor, v.offset + GRID_W - 1, [list(d) for d in v.ap[:2]] + [[-1, GRID_W]])

        def bcast(v, at, n):
            return bass.AP(v.tensor, at, [[0, P], [1, n]])

        block = ctx.enter_context(nc.Block())

        @block.sync
        def _(sp):
            sp.dma_start(x[:], x_in.rearrange("b (m p) d -> p (b m) d", p=P)).then_inc(x_landed, 16)
            sp.dma_start(cst[:], consts).then_inc(consts_landed, 16)
            sp.dma_start(vec_rows[0:D_IN // P, :], b_in.rearrange("l (b p) -> (l b) p", p=P)).then_inc(vec_landed, 16)
            sp.dma_start(vec_rows[D_IN // P:n_vec, :], norm1_g.rearrange("l (b p) -> (l b) p", p=P)).then_inc(vec_landed, 16)

            def chunk_source(n):
                if n < N_IN:
                    return w_in[0, :, n * CW:(n + 1) * CW].rearrange("(k p) n -> p k n", p=P)
                n -= N_IN
                if n < N_UP:
                    w = (w_up_a, w_up_b)[n % 2]
                    return w[0, :, n // 2 * 512:(n // 2 + 1) * 512].rearrange("(k p) n -> p k n", p=P)
                n -= N_UP
                return w_out[0, :, n * CW:(n + 1) * CW].rearrange("(k p) n -> p k n", p=P)

            for n in range(PRE):
                if n >= SLOTS:
                    sp.wait_ge(chunk_used, n - SLOTS + 1)
                src = chunk_source(n)
                dst = ring[:, slot_of(n), :].rearrange("p (k n) -> p k n", n=src.shape[2])
                sp.dma_start(dst, src).then_inc(landed[slot_of(n)], 16)
                if n == 3:
                    sp.dma_start(v_bias[:, 0:NA_W], bcast(b_in, 2 * NA_W, NA_W)).then_inc(attn_small_landed, 16)
                    sp.dma_start(v_bias[:, NA_W:], bcast(b_in, 4 * NA_W + P, P)).then_inc(attn_small_landed, 16)
                    sp.dma_start(sink_b[:], bcast(swa_sinks, 0, HEADS)).then_inc(attn_small_landed, 16)
                    for r in range(2):
                        for hd in range(HEADS):
                            at = hd * RPB + (NA_ROWS - 1 - 2 - r) * RPB_W + NA_COLS - 1
                            src = bass.AP(na_rpb.tensor, at - (GRID_W - 1), [[1, GRID_W], [RPB_W, DR], [1, GRID_W]])
                            dst = na_bias[r * GRID_W:(r + 1) * GRID_W, hd, :].rearrange("p (a c) -> p a c", c=GRID_W)
                            sp.dma_start(dst, src).then_inc(bias_landed, 16)
                if n == 8:
                    sp.dma_start(g2_b[:], bcast(norm2_g, 0, D)).then_inc(route_landed, 16)
                    sp.dma_start(wr[:], w_router[0].rearrange("(k p) e -> p k e", p=P)).then_inc(route_landed, 16)
                    sp.dma_start(br[:], b_router.rearrange("l e -> e l")).then_inc(route_landed, 16)
                if n == PRE - 2:
                    sp.wait_ge(scores_done, UNITS)
                    sp.dma_start(gf_b, bcast(final_g, 0, D)).then_inc(final_g_landed, 16)
                    sp.dma_start(b1_sb, b1[0]).then_inc(expert_bias_landed, 16)
                    sp.dma_start(b2_sb, b2[0]).then_inc(expert_bias_landed, 16)

            def load_expert(e, blk):
                one = bass.ds(e, 1)
                for c in range(BLK):
                    sp.wait_ge(chunk_used, blk * BLK + PRE + c - SLOTS + 1)
                    s = expert_slot(c)[0]
                    if c < W1_CH:
                        src = w1[0, one, c * P:(c + 1) * P, :].rearrange("e p n -> p (e n)")
                        dst = ring[:, s, :]
                    else:
                        r0 = (c - W1_CH) * 2 * P
                        src = w2[0, one, r0:r0 + 2 * P, :].rearrange("e (j p) n -> p (e j) n", p=P)
                        dst = ring[:, s, :].rearrange("p (j n) -> p j n", j=2)
                    sp.dma_start(dst, src).then_inc(landed[s], 16)

            with sp.Fori(0, E) as blk:
                load_expert(blk, blk)
            sp.wait_ge(ctrl_ready, 1)
            n_over = sp.value_load(ctrl[0:1, OVER:OVER + 1], min_val=0, max_val=OVER_MAX)
            with sp.Fori(0, OVER_MAX) as j:
                with sp.If(j < n_over):
                    e = sp.value_load(ctrl[0:1, bass.ds(j, 1)], min_val=0, max_val=E - 1)
                    load_expert(e, j + E)
                sp.nop()
            for m in range(MT):
                sp.wait_ge(out_ready, m + 1)
                sp.dma_start(out[0, m * P:(m + 1) * P, :], h2[:, m, :]).then_inc(out_stored, 16)
            sp.wait_ge(out_stored, 16 * MT)

        @block.gpsimd
        def _(pool):
            pool.memset(ones[:], 1.0).then_inc(ones_set, 1)
            pool.memset(zeros[:], 0.0).then_inc(ones_set, 1)
            pool.memset(minus_half[:], -0.5).then_inc(pool_step, 1)
            pool.wait_ge(pool_step, 1)

            def power(n):
                pool.wait_ge(msq_ready, n + 1)
                pool.tensor_tensor(rstd[:, n, :], msq[:, n, :], minus_half[:], ALU.pow).then_inc(rstd_ready, 1)

            power(0)
            pool.wait_ge(bias_landed, 16 * 2 * HEADS)
            pool.wait_ge(consts_landed, 16)
            for hd in range(HEADS):
                v = na_bias[:, hd, :].rearrange("p (a c) -> p a c", c=GRID_W)
                mask = C("na_mask").rearrange("p (o c) -> p o c", o=1).to_broadcast([P, DR, GRID_W])
                pool.tensor_tensor(v, v, mask, ALU.add).then_inc(masked_bias, 1)
            power(1)
            power(2)

        @block.tensor
        def _(pe):
            pe.wait_ge(consts_landed, 16)
            pe.wait_ge(vec_landed, 32)
            pe.transpose(bank[:, 4, 0:n_vec], vec_rows[0:n_vec, :], C("ident")[0:n_vec, 0:n_vec]).then_inc(vec_done, 1)
            for m in range(MT):
                pe.wait_ge(h_ready, m + 1)
                for a in range(2):
                    for j in range(4):
                        k = 4 * a + j
                        last = pe.transpose(quarter(2 * m + a)[:, j, :], h[:, m, k * P:(k + 1) * P], C("ident"))
                    last.then_inc(hT_done, 1)
            pe.wait_ge(hT_ready, 2 * MT)

            def project(c):
                if c >= 3:
                    if c - 3 < GATE_C:
                        pe.wait_ge(proj_read_dve, c - 2)
                    else:
                        pe.wait_ge(proj_read_act, c - 3 - GATE_C + 1)
                if c % 3 == BK and c > GATE_C:
                    pe.wait_ge(rope_ready, 1)
                w = ring[:, slot_of(c), :].rearrange("p (k n) -> p k n", n=CW)
                pe.wait_ge(landed[slot_of(c)], landings(c))
                dst = half_(c % 3)
                for a in range(2):
                    for k in range(KD):
                        st = dict(start=k == 0, stop=k == KD - 1)
                        if c in (4, 5):
                            last = pe.matmul(dst[:, a, :], hT[:, k, a * P:(a + 1) * P], w[:, k, :], **st)
                        elif c == 8 and a == 1:
                            continue
                        else:
                            last = pe.matmul(dst[:, a, :], w[:, k, a * P:(a + 1) * P], hT[:, k, :], **st)
                if c == 8:
                    for m in range(MT):
                        for k in range(KD):
                            last = pe.matmul(dst[:, 1, m * P:(m + 1) * P], hT[:, k, m * P:(m + 1) * P],
                                             w[:, k, P:2 * P], start=k == 0, stop=k == KD - 1)
                last.then_inc(chunk_used, 1)

            def scores(u):
                pair = u % 4
                if u == 0:
                    pe.wait_ge(proj_read_dve, 4)
                if u == 4:
                    pe.wait_ge(rope_ready, 1)
                if u:
                    pe.wait_ge(max_ready, u)
                for qt in range(MT):
                    for i in range(2):
                        rows = slice(DH * i, DH * i + DH)
                        q, k = (qaT, kaT[:, pair, :]) if u < 4 else (qbT[:], kbT[:, pair // 2, :])
                        last = pe.matmul(bank[:, BS + i, qt * T:(qt + 1) * T], q[rows, pair, qt * P:(qt + 1) * P],
                                         k[rows, :], start=True, stop=True)
                last.then_inc(scores_done, 1)

            def attend(u):
                pair = u % 4
                pe.wait_ge(prob_ready, u + 1)
                if u == ROPE_U:
                    pe.wait_ge(rope_ready, 1)
                for i in range(2):
                    for kt in range(2):
                        for qt in range(MT):
                            last = pe.transpose(bank[:, BT + i, kt * T + qt * P:kt * T + (qt + 1) * P],
                                                prob[u % 2][:, i, qt, kt * P:(kt + 1) * P], C("ident"))
                last.then_inc(probT_done, 1)
                pe.wait_ge(probT_ready, u + 1)
                if u == 0:
                    pe.wait_ge(proj_read_dve, 6)
                if u:
                    pe.wait_ge(o_ready, u)
                for kt in range(2):
                    for i in range(2):
                        col = (2 * pair + i) * DH if u < 4 else NA_W + pair // 2 * DH
                        last = pe.matmul(bank[DH * i:DH * i + DH, BO, 0:T], v_sb[:, kt, col:col + DH],
                                         probT[:, i, kt, :], start=kt == 0, stop=kt == 1)
                last.then_inc(o_done, 1)

            def rotate():
                pe.wait_ge(proj_read_dve, 9)
                pe.wait_ge(o_ready, ROPE_U)
                for b in range(4):
                    pe.matmul(half_(BT + b // 2)[:, b % 2, :], C("rot"), qbT[:, b, :], start=True, stop=True)
                for g in range(KV_HEADS):
                    pe.matmul(half_(BO)[:, g, :], C("dup")[:, g * P:(g + 1) * P], kraw[:], start=True, stop=True)
                    last = pe.matmul(half_(BK)[:, g, :], C("dup_rot")[:, g * P:(g + 1) * P], kraw[:],
                                     start=True, stop=True)
                last.then_inc(rope_done, 1)

            for c in range(FIRST_U):
                project(c)
            for c in range(FIRST_U, N_IN):
                u = c - FIRST_U
                if u == ROPE_U:
                    rotate()
                if u < UNITS:
                    scores(u)
                project(c)
                if u < UNITS:
                    attend(u)

            pe.wait_ge(o_ready, UNITS)
            pe.wait_ge(proj_read_act, N_IN - GATE_C)
            for n in range(N_UP):
                c, branch = N_IN + n, n % 2
                w = ring[:, slot_of(c), :].rearrange("p (k n) -> p k n", n=512)
                pe.wait_ge(landed[slot_of(c)], landings(c))
                for j in range(4):
                    for k in range(4):
                        last = pe.matmul(half_(2 * n + j // 2)[:, j % 2, :], w[:, k, j * P:(j + 1) * P],
                                         oT[:, 4 * branch + k, :], start=k == 0, stop=k == 3)
                last.then_inc(chunk_used, 1)

            for n in range(N_OUT):
                c = N_IN + N_UP + n
                w = ring[:, slot_of(c), :].rearrange("p (k n) -> p k n", n=CW)
                pe.wait_ge(landed[slot_of(c)], landings(c))
                for m in range(MT):
                    for k in range(KD):
                        if k in (0, 4):
                            pe.wait_ge(merged_ready, k // 4 + 1)
                        last = pe.matmul(half_(n)[:, m, :], merged[:, k, m * P:(m + 1) * P], w[:, k, :],
                                         start=k == 0, stop=k == KD - 1)
                last.then_inc(chunk_used, 1)

            for m in range(MT):
                pe.wait_ge(h2_ready, m + 1)
                for a in range(2):
                    for j in range(4):
                        k = 4 * a + j
                        last = pe.transpose(quarter(4 + 2 * m + a)[:, j, :], h2[:, m, k * P:(k + 1) * P], C("ident"))
                    last.then_inc(h2T_done, 1)
            pe.wait_ge(h2T_ready, 2 * MT)
            pe.wait_ge(route_landed, 48)
            for k in range(KD):
                last = pe.matmul(bank[0:E, 4, 0:T], wr[:, k, :], h2T[:, k, :], start=k == 0, stop=k == KD - 1)
            last.then_inc(logT_done, 1)
            pe.wait_ge(x2_ready, N_OUT)
            for m in range(MT):
                for a in range(2):
                    pe.matmul(bank[:, 2 * m + a, :], C("ident"), x[:, m, a * 512:(a + 1) * 512],
                              start=True, stop=False, skip_group_check=True)
            pe.wait_ge(logT_ready, 1)
            for m in range(MT):
                last = pe.transpose(bank[:, 5, m * E:(m + 1) * E], logT[:, m * P:(m + 1) * P], C("ident")[0:E, 0:E])
            last.then_inc(log_done, 1)
            pe.wait_ge(chosen_ready, 1)
            pe.wait_ge(ones_set, 2)
            pe.matmul(bank[:, 6, 0:E], C("before"), chosen[:, 0, :], start=True, stop=True)
            pe.matmul(bank[:, 6, E:2 * E], ones[:], chosen[:, 0, :], start=True, stop=False)
            pe.matmul(bank[:, 6, E:2 * E], C("before"), chosen[:, 1, :], start=False, stop=True)
            for m in range(MT):
                last = pe.matmul(bank[0:E, 7, 0:1], chosen[:, m, :], ones[:, 0:1], start=m == 0, stop=m == 1)
            last.then_inc(count_done, 1)

            def gather():
                for m in range(MT):
                    for a in range(2):
                        last = pe.matmul(bank[CAP * a:CAP * (a + 1), BX, :], pick[:, m, :],
                                         h2[:, m, a * 512:(a + 1) * 512], start=m == 0, stop=m == 1)
                last.then_inc(xg_done, 1)

            def turn(dst, src, n, done):
                for j in range(n):
                    last = pe.transpose(quarter(dst)[:, j, :], src(j), C("ident"))
                last.then_inc(done, 1)

            turn_gathered = lambda: turn(BX, lambda j: xg[:, j * P:(j + 1) * P], 4, xgT_done)

            pe.wait_ge(pick_ready, 1)
            gather()
            pe.wait_ge(xg_ready, 1)
            turn_gathered()
            pe.wait_ge(extra_ready, 1)
            pe.matmul(bank[0:E, 7, 1:2], C("before")[0:E, 0:E], extra[:, 0:1], start=True, stop=True).then_inc(start_done, 1)
            pe.wait_ge(place_ready, 1)
            for m in range(MT):
                pe.transpose(bank[0:E, 4, m * P:(m + 1) * P], share[:, m, 0:E], C("ident"))
                last = pe.transpose(bank[0:E, 4, (2 + m) * P:(3 + m) * P], place[:, m, 0:E], C("ident"))
            last.then_inc(tr_done, 1)
            pe.wait_ge(tr_ready, 2)
            over = is_exp[:, E:NBC]
            for m in range(MT):
                tok = slice(m * P, (m + 1) * P)
                pe.matmul(bank[:, 5, m * OVER:(m + 1) * OVER], placeT[:, tok], over, start=True, stop=False)
                pe.matmul(bank[:, 5, m * OVER:(m + 1) * OVER], ones[0:E, :], sel_off[:], start=False, stop=True)
                pe.matmul(bank[:, 5, (2 + m) * OVER:(3 + m) * OVER], shareT[:, tok], over, start=True, stop=True)
            pe.matmul(bank[0:1, 5, 4 * OVER:5 * OVER], C("expert")[0:E, :], over, start=True, stop=True)
            pe.matmul(bank[0:1, 5, 5 * OVER:5 * OVER + 1], extra[:, 0:1], ones[0:E, 0:1],
                      start=True, stop=True).then_inc(list_done, 1)
            pe.wait_ge(expert_bias_landed, 32)
            for m in range(MT):
                for a in range(2):
                    pe.matmul(bank[:, 2 * m + a, :], shareT[:, m * P:(m + 1) * P], b2_sb[:, a * 512:(a + 1) * 512],
                              start=False, stop=False, skip_group_check=True)

            def expert_block(b):
                pe.wait_ge(xgT_ready, b + 1)
                pe.wait_ge(b1_pick_ready, b + 1)
                pe.wait_ge(scatT_ready, b + 1)
                parts = [(BG, 0), (BG, 1), (BU, 0), (BU, 1)]
                for q, (bk, a) in enumerate(parts):
                    pe.matmul(bank[CAP * a:CAP * (a + 1), bk, :], b1_pick[:], b1_sb[:, q * 512:(q + 1) * 512],
                              start=True, stop=False)
                for k in range(W1_CH):
                    s, count = expert_slot(k)
                    pe.wait_ge(landed[s], b * 16 + count)
                    kT = xgT[:, (k % 4) * P + k // 4 * CAP:(k % 4) * P + (k // 4 + 1) * CAP]
                    for q, (bk, a) in enumerate(parts):
                        last = pe.matmul(bank[CAP * a:CAP * (a + 1), bk, :], kT, ring[:, s, q * 512:(q + 1) * 512],
                                         start=False, stop=k == W1_CH - 1)
                    last.then_inc(chunk_used, 1)
                pe.wait_ge(pick_ready, b + 2)
                gather()
                pe.wait_ge(hid_ready, b + 1)
                turn(BH, lambda j: hid[:, j * P:(j + 1) * P], 4, hidT_done)
                pe.wait_ge(pick_g_ready, b + 1)
                turn(BU, lambda m: pick_g[:, m, :], MT, scatT_done)
                pe.wait_ge(xg_ready, b + 2)
                turn_gathered()
                pe.wait_ge(hidT_ready, b + 1)
                for f in range(2 * W2_CH):
                    s, count = expert_slot(W1_CH + f // 2)
                    if f % 2 == 0:
                        pe.wait_ge(landed[s], b * 16 + count)
                    fT = hidT[:, (f % 4) * P + f // 4 * CAP:(f % 4) * P + (f // 4 + 1) * CAP]
                    for a in range(2):
                        last = pe.matmul(bank[CAP * a:CAP * (a + 1), BH, :], fT,
                                         ring[:, s, f % 2 * D + a * 512:f % 2 * D + (a + 1) * 512],
                                         start=f == 0, stop=f == 2 * W2_CH - 1)
                    if f % 2:
                        last.then_inc(chunk_used, 1)
                pe.wait_ge(down_ready, b + 1)
                pe.wait_ge(scatT_ready, b + 2)
                for m in range(MT):
                    for a in range(2):
                        rows = slice(CAP * a, CAP * (a + 1))
                        last = pe.matmul(bank[:, 2 * m + a, :], scatT[rows, m * P:(m + 1) * P], down_s[rows, :],
                                         start=False, stop=False, skip_group_check=True)
                last.then_inc(scatter_done, 1)

            pe.sem_inc(scatT_done, 1)
            pe.sem_inc(scatter_done, 1)
            pe.wait_ge(ctrl_ready, 1)
            with pe.Fori(0, E) as b:
                expert_block(b)
            n_over = pe.value_load(ctrl[0:1, OVER:OVER + 1], min_val=0, max_val=OVER_MAX)
            with pe.Fori(0, OVER_MAX) as j:
                with pe.If(j < n_over):
                    expert_block(j + E)
                pe.nop()
            for m in range(MT):
                for a in range(2):
                    last = pe.matmul(bank[:, 2 * m + a, :], zeros[0:1, 0:P], zeros[0:1, :],
                                     start=False, stop=True, skip_group_check=True)
            last.then_inc(y_done, 1)

        @block.vector
        def _(dve):
            ch = Chain(dve, dve_step)

            def square_sum(n, m):
                dve.tensor_tensor_reduce(out=(h if n == 0 else h2)[:, m, :], in0=x[:, m, :], in1=x[:, m, :], scale=1.0,
                                         scalar=0.0, op0=ALU.mult, op1=ALU.add,
                                         accum_out=ssq[:, n, m:m + 1]).then_inc(ssq_dve, 1)

            def mean_square(n):
                square_sum(n, 0)
                dve.wait_ge(ssq_dve, n + 1)
                dve.wait_ge(ssq_act, n + 1)
                dve.tensor_scalar(msq[:, n, :], ssq[:, n, :], 1.0 / D, EPS, ALU.mult, ALU.add).then_inc(msq_ready, 1)
                dve.wait_ge(rstd_ready, n + 1)

            dve.wait_ge(ones_set, 2)
            dve.wait_ge(x_landed, 16)
            mean_square(0)
            for m in range(MT):
                dve.tensor_scalar(h[:, m, :], x[:, m, :], rstd[:, 0, m:m + 1], None, ALU.mult).then_inc(h_ready, 1)
            dve.wait_ge(vec_done, 1)
            dve.tensor_copy(vec[:], bank[:, 4, 0:n_vec]).then_inc(vec_ready, 1)
            dve.wait_ge(vec_ready, 1)
            for g in range(2 * MT):
                m, a = g // 2, g % 2
                dve.wait_ge(hT_done, g + 1)
                g1 = vec[:, D_IN // P + 4 * a:D_IN // P + 4 * a + 4].rearrange("p (k o) -> p k o", o=1)
                dve.tensor_tensor(hT[:, 4 * a:4 * a + 4, m * P:(m + 1) * P], quarter(g),
                                  g1.to_broadcast([P, 4, P]), ALU.mult).then_inc(hT_ready, 1)

            def read_projection(c):
                dve.wait_ge(chunk_used, c + 1)
                src = half_(c % 3)
                if c in (4, 5):
                    col = slice((c - 4) * CW, (c - 3) * CW)
                    bias = v_bias[:, col].rearrange("p (o n) -> p o n", o=1).to_broadcast([P, MT, CW])
                    last = dve.tensor_tensor(v_sb[:, :, col], src, bias, ALU.add)
                elif c == 8:
                    dve.tensor_scalar(kraw[:], src[:, 0, :], vec[:, 2 * c:2 * c + 1], None, ALU.add)
                    bias = v_bias[:, NA_W:].rearrange("p (o n) -> p o n", o=1).to_broadcast([P, MT, P])
                    last = dve.tensor_tensor(v_sb[:, :, NA_W:], src[:, 1, :].rearrange("p (m n) -> p m n", m=MT),
                                             bias, ALU.add)
                else:
                    for a in range(2):
                        b = 2 * c + a
                        bias = vec[:, b:b + 1]
                        if c < 2:
                            last = dve.tensor_scalar(qaT[:, b, :].rearrange("p (r c) -> p r c", c=GRID_W),
                                                     from_right(src[:, a, :]), bias, SCALE, ALU.add, ALU.mult)
                        elif c < 4:
                            last = dve.tensor_scalar(kaT[:, b - 4, :], src[:, a, :], bias, None, ALU.add)
                        else:
                            last = dve.tensor_scalar(qbT[:, b - 12, :], src[:, a, :], bias, SCALE, ALU.add, ALU.mult)
                last.then_inc(proj_read_dve, 1)

            def rotary():
                two = lambda n: C(n).rearrange("p (o t) -> p o t", o=1).to_broadcast([P, 2, T])
                dve.wait_ge(rope_done, 1)
                for b in range(2):
                    q = qbT[:, 2 * b:2 * b + 2, :]
                    dve.tensor_tensor(rtmp[:], half_(BT + b), two("sin"), ALU.mult)
                    ch.link(dve.tensor_tensor(q, q, two("cos"), ALU.mult))
                    ch.link(dve.tensor_tensor(q, q, rtmp[:], ALU.add))
                dve.tensor_tensor(rtmp[:], half_(BO), two("cos"), ALU.mult)
                ch.link(dve.tensor_tensor(rtmp2[:], half_(BK), two("sin"), ALU.mult))
                dve.tensor_tensor(kbT, rtmp[:], rtmp2[:], ALU.add).then_inc(rope_ready, 1)

            def softmax(u):
                pair, s = u % 4, prob[u % 2]
                dve.wait_ge(scores_done, u + 1)
                if u >= 2:
                    dve.wait_ge(probT_done, u - 1)
                if u < 4:
                    if u == 0:
                        dve.wait_ge(masked_bias, HEADS)
                    for qt in range(MT):
                        bias = na_bias[:, 2 * pair:2 * pair + 2, (2 - 2 * qt) * GRID_W:(2 - 2 * qt + ROWS) * GRID_W]
                        last = dve.tensor_tensor(s[:, :, qt, :], bank[:, BS:BS + 2, qt * T:(qt + 1) * T], bias, ALU.add)
                else:
                    mask = C("swa_mask").rearrange("p (o t) -> p o t", o=1).to_broadcast([P, 2, MT * T])
                    last = dve.tensor_tensor(s[:].rearrange("p i m t -> p i (m t)"), bank[:, BS:BS + 2, :], mask, ALU.add)
                ch.link(last)
                ch.link(dve.tensor_reduce(mx[:], s[:], AX.X, ALU.max))
                sink = sink_b[:, 2 * pair:2 * pair + 2].rearrange("p (i o) -> p i o", o=1).to_broadcast([P, 2, MT])
                if u >= 4:
                    ch.link(dve.tensor_tensor(mx[:], mx[:], sink, ALU.max))
                    ch.link(dve.tensor_tensor(e_sink[:], sink, mx[:], ALU.subtract))
                dve.tensor_scalar(neg_mx[:], mx[:], -1.0, None, ALU.mult).then_inc(max_ready, 1)
                dve.wait_ge(exp_ready, u + 1)
                if u >= 4:
                    ch.link(dve.tensor_tensor(den[:], den[:], e_sink[:], ALU.add))
                ch.link(dve.reciprocal(den[:], den[:]))
                for i in range(2):
                    inv = den[:, i, :].rearrange("p (m o) -> p m o", o=1).to_broadcast([P, MT, T])
                    last = dve.tensor_tensor(s[:, i, :, :], s[:, i, :, :], inv, ALU.mult)
                last.then_inc(prob_ready, 1)

            def read_output(u):
                dve.wait_ge(o_done, u + 1)
                dst, src = oT[:, u, :], bank[:, BO, 0:T]
                if u < 4:
                    dst, src = dst.rearrange("p (r c) -> p r c", c=GRID_W), from_right(src)
                dve.tensor_copy(dst, src).then_inc(o_ready, 1)

            for c in range(FIRST_U):
                if c == 4:
                    dve.wait_ge(attn_small_landed, 48)
                read_projection(c)
            for c in range(FIRST_U, FIRST_U + UNITS):
                u = c - FIRST_U
                if u == ROPE_U:
                    rotary()
                softmax(u)
                if c < GATE_C:
                    read_projection(c)
                read_output(u)

            dve.wait_ge(sig_ready, 2)
            for hf in range(2):
                ga, gb = gates[:, 4 * hf:4 * hf + 4, :], gates[:, KD + 4 * hf:KD + 4 * hf + 4, :]
                lifted = lambda b: bank[:, b:b + 2, :].rearrange("p b (a t) -> p (b a) t", t=T)
                dve.wait_ge(chunk_used, N_IN + 2 * hf + 1)
                dve.tensor_tensor(ga, ga, lifted(4 * hf), ALU.mult)
                dve.wait_ge(chunk_used, N_IN + 2 * hf + 2)
                ch.link(dve.tensor_tensor(gb, gb, lifted(4 * hf + 2), ALU.mult))
                dve.tensor_tensor(ga, ga, gb, ALU.add).then_inc(merged_ready, 1)
            for n in range(N_OUT):
                xs = x[:, :, n * CW:(n + 1) * CW]
                dve.wait_ge(chunk_used, N_IN + N_UP + n + 1)
                dve.tensor_tensor(xs, xs, half_(n), ALU.add).then_inc(x2_ready, 1)
            dve.wait_ge(x2_ready, N_OUT)
            mean_square(1)
            dve.wait_ge(route_landed, 48)
            for m in range(MT):
                dve.scalar_tensor_tensor(out=h2[:, m, :], in0=x[:, m, :], scalar=rstd[:, 1, m:m + 1], in1=g2_b[:],
                                         op0=ALU.mult, op1=ALU.mult).then_inc(h2_ready, 1)
            for g in range(2 * MT):
                m, a = g // 2, g % 2
                dve.wait_ge(h2T_done, g + 1)
                dve.tensor_copy(h2T[:, 4 * a:4 * a + 4, m * P:(m + 1) * P], quarter(4 + g)).then_inc(h2T_ready, 1)
            dve.wait_ge(logT_done, 1)
            dve.tensor_scalar(logT, bank[0:E, 4, 0:T], br[:], None, ALU.add).then_inc(logT_ready, 1)
            dve.wait_ge(log_done, 1)
            ch.link(dve.tensor_copy(logit[:], bank[:, 5, 0:MT * E].rearrange("p (m e) -> p m e", m=MT)))
            for m in range(MT):
                last = dve.max(top8[:, m, :], logit[:, m, :])
            ch.link(last)
            dve.tensor_scalar(neg_top[:], top8[:, :, 0], -1.0, None, ALU.mult).then_inc(top_ready, 1)
            for m in range(MT):
                fourth = top8[:, m, TOPK - 1:TOPK]
                dve.tensor_scalar(above[:, m, :], logit[:, m, :], fourth, None, ALU.is_gt)
                last = dve.tensor_scalar(equal[:, m, :], logit[:, m, :], fourth, None, ALU.is_equal)
            ch.link(last)
            ch.link(dve.tensor_reduce(n_gt[:], above[:], AX.X, ALU.add))
            ch.link(dve.tensor_scalar(n_gt[:], n_gt[:], -1.0, float(TOPK), ALU.mult, ALU.add))
            for m in range(MT):
                last = dve.tensor_tensor_scan(nth[:, m, :], ones[:, 0:E], equal[:, m, :], 0.0, ALU.mult, ALU.add)
            ch.link(last)
            for m in range(MT):
                last = dve.scalar_tensor_tensor(out=equal[:, m, :], in0=nth[:, m, :], scalar=n_gt[:, m:m + 1],
                                                in1=equal[:, m, :], op0=ALU.is_le, op1=ALU.mult)
            ch.link(last)
            dve.tensor_tensor(chosen[:], above[:], equal[:], ALU.add).then_inc(chosen_ready, 1)
            dve.wait_ge(chosen_ready, 1)
            ch.link(dve.memset(place[:, :, E:NBC], -1.0))
            dve.wait_ge(top_exp, 1)
            ch.link(dve.tensor_tensor(share[:, :, 0:E], share[:, :, 0:E], chosen[:], ALU.mult))
            ch.link(dve.tensor_reduce(g_sum[:], share[:, :, 0:E], AX.X, ALU.add))
            ch.link(dve.reciprocal(g_sum[:], g_sum[:]))
            inv = g_sum[:].rearrange("p (m o) -> p m o", o=1).to_broadcast([P, MT, E])
            ch.link(dve.tensor_tensor(share[:, :, 0:E], share[:, :, 0:E], inv, ALU.mult))
            dve.wait_ge(count_done, 1)
            rank = bank[:, 6, 0:MT * E].rearrange("p (m e) -> p m e", m=MT)
            ch.link(dve.scalar_tensor_tensor(out=place[:, :, 0:E], in0=rank, scalar=FAR, in1=chosen[:],
                                             op0=ALU.add, op1=ALU.mult))
            dve.tensor_scalar(place[:, :, 0:E], place[:, :, 0:E], -FAR, None, ALU.add).then_inc(place_ready, 1)
            dve.wait_ge(place_ready, 1)

            def make_pick(col):
                for m in range(MT):
                    last = dve.tensor_scalar(pick[:, m, :], C("slot")[:, 0:CAP], place[:, m, col], None, ALU.is_equal)
                last.then_inc(pick_ready, 1)

            def make_b1_pick(col):
                dve.tensor_copy(b1_pick[:], is_exp[:, col].to_broadcast([E, CAP])).then_inc(b1_pick_ready, 1)

            make_pick(bass.ds(0, 1))
            ch.link(dve.tensor_copy(is_exp[:, 0:E], C("ident")[0:E, 0:E]))
            make_b1_pick(bass.ds(0, 1))
            count = bank[0:E, 7, 0:1]
            dve.tensor_scalar(extra[:, 1:2], count, float(CAP), None, ALU.is_gt)
            ch.link(dve.tensor_scalar(extra[:, 2:3], count, float(2 * CAP), None, ALU.is_gt))
            dve.tensor_scalar(extra[:, 3:4], count, float(3 * CAP), None, ALU.is_gt)
            ch.link(dve.tensor_tensor(extra[:, 1:2], extra[:, 1:2], extra[:, 2:3], ALU.add))
            dve.tensor_tensor(extra[:, 0:1], extra[:, 1:2], extra[:, 3:4], ALU.add).then_inc(extra_ready, 1)
            dve.wait_ge(start_done, 1)
            over = is_exp[:, E:NBC]
            ch.link(dve.tensor_copy(extra[:, 1:2], bank[0:E, 7, 1:2]))
            ch.link(dve.tensor_scalar(from_j[:], C("over")[0:E, :], extra[:, 1:2], None, ALU.subtract))
            dve.tensor_scalar(sel_off[:], from_j[:], 0.0, None, ALU.is_ge)
            ch.link(dve.tensor_scalar(over, from_j[:], extra[:, 0:1], None, ALU.is_lt))
            ch.link(dve.tensor_tensor(over, over, sel_off[:], ALU.mult))
            ch.link(dve.tensor_scalar(from_j[:], from_j[:], 1.0, -float(CAP), ALU.add, ALU.mult))
            dve.tensor_tensor(sel_off[:], from_j[:], over, ALU.mult).then_inc(tr_ready, 1)
            dve.wait_ge(tr_done, 1)
            dve.tensor_copy(shareT, bank[0:E, 4, 0:T])
            dve.tensor_copy(placeT, bank[0:E, 4, T:2 * T]).then_inc(tr_ready, 1)
            dve.wait_ge(list_done, 1)
            lists = bank[:, 5, 0:4 * OVER].rearrange("p (a m j) -> p a m j", a=2, m=MT)
            dve.tensor_copy(place[:, :, E:NBC], lists[:, 0])
            dve.tensor_copy(share[:, :, E:NBC], lists[:, 1])
            dve.tensor_copy(ctrl[:], bank[0:1, 5, 4 * OVER:5 * OVER + 1]).then_inc(ctrl_ready, 1)
            dve.wait_ge(ctrl_ready, 1)
            loop_base = ch.n

            STEPS = 2

            def expert_block(b):
                one, nxt = bass.ds(b, 1), bass.ds(b + 1, 1)
                ch.base, ch.n = b * STEPS + loop_base, 0
                dve.wait_ge(scatT_done, b + 1)
                for m in range(MT):
                    last = dve.tensor_scalar(pick_g[:, m, :], C("slot"), place[:, m, one], share[:, m, one],
                                             ALU.is_equal, ALU.mult)
                last.then_inc(pick_g_ready, 1)
                dve.wait_ge(xg_done, b + 1)
                make_pick(nxt)
                dve.wait_ge(chunk_used, b * BLK + PRE + W1_CH)
                dve.tensor_scalar(gate_s, bank[:, BG, :], LIMIT, None, ALU.min).then_inc(gate_ready, 1)
                ch.link(dve.tensor_scalar(up_s, bank[:, BU, :], LIMIT, -LIMIT, ALU.min, ALU.max))
                dve.wait_ge(gate_ready, b + 1)
                ch.link(dve.scalar_tensor_tensor(out=up_s, in0=up_s, scalar=1.0, in1=gate_s, op0=ALU.add, op1=ALU.mult))
                dve.wait_ge(sigm_ready, b + 1)
                dve.tensor_tensor(hid, up_s, sig_s, ALU.mult).then_inc(hid_ready, 1)
                make_b1_pick(nxt)
                dve.wait_ge(hidT_done, b + 1)
                dve.tensor_copy(hidT, bank[:, BH, :]).then_inc(hidT_ready, 1)
                dve.wait_ge(chunk_used, b * BLK + PRE + BLK)
                dve.wait_ge(scatter_done, b + 1)
                dve.tensor_copy(down_s, bank[:, BH, :]).then_inc(down_ready, 1)
                assert ch.n == STEPS

            with dve.Fori(0, E) as b:
                expert_block(b)
            n_over = dve.value_load(ctrl[0:1, OVER:OVER + 1], min_val=0, max_val=OVER_MAX)
            with dve.Fori(0, OVER_MAX) as j:
                with dve.If(j < n_over):
                    expert_block(j + E)
                dve.nop()
            dve.wait_ge(y_done, 1)
            dve.wait_ge(final_g_landed, 16)
            for m in range(MT):
                dve.tensor_copy(x[:, m, :], bank[:, 2 * m:2 * m + 2, :].rearrange("p b n -> p (b n)")).then_inc(x2_ready, 1)
            dve.wait_ge(x2_ready, N_OUT + MT)
            mean_square(2)
            for m in range(MT):
                dve.scalar_tensor_tensor(out=h2[:, m, :], in0=x[:, m, :], scalar=rstd[:, 2, m:m + 1], in1=gf_b,
                                         op0=ALU.mult, op1=ALU.mult).then_inc(out_ready, 1)

        @block.scalar
        def _(act):
            def square_sum(n, dst):
                act.activation(dst, x[:, 1, :], ACT.Square, accum_out=ssq[:, n, 1:2]).then_inc(ssq_act, 1)

            act.wait_ge(x_landed, 16)
            square_sum(0, h[:, 1, :])
            act.wait_ge(vec_ready, 1)
            for c in range(FIRST_U, N_IN):
                u = c - FIRST_U
                if u < UNITS:
                    s = prob[u % 2]
                    act.wait_ge(max_ready, u + 1)
                    if u >= 4:
                        act.activation(e_sink[:], e_sink[:], ACT.Exp)
                    for i in range(2):
                        for qt in range(MT):
                            last = act.activation(s[:, i, qt, :], s[:, i, qt, :], ACT.Exp,
                                                  bias=neg_mx[:, i, qt:qt + 1], accum_out=den[:, i, qt:qt + 1])
                    last.then_inc(exp_ready, 1)
                if c >= GATE_C:
                    act.wait_ge(chunk_used, c + 1)
                    for a in range(2):
                        b = 2 * (c - GATE_C) + a
                        last = act.activation(gates[:, b, :], half_(c % 3)[:, a, :],
                                              ACT.Identity if u < UNITS else ACT.Sigmoid, bias=vec[:, 2 * c + a:2 * c + a + 1])
                    last.then_inc(proj_read_act, 1)
                if u < UNITS:
                    act.wait_ge(probT_done, u + 1)
                    if u:
                        act.wait_ge(o_done, u)
                    act.activation(probT[:].rearrange("p i k t -> p (i k t)"),
                                   bank[:, BT:BT + 2, :].rearrange("p b n -> p (b n)"), ACT.Identity).then_inc(probT_ready, 1)
                if u == UNITS - 1:
                    n = 2 * (c - GATE_C + 1)
                    act.wait_ge(proj_read_act, c - GATE_C + 1)
                    act.activation(gates[:, 0:n, :], gates[:, 0:n, :], ACT.Sigmoid).then_inc(sig_ready, 1)
            act.wait_ge(proj_read_act, N_IN - GATE_C)
            act.sem_inc(sig_ready, 1)
            act.wait_ge(x2_ready, N_OUT)
            square_sum(1, h2[:, 1, :])
            act.wait_ge(top_ready, 1)
            for m in range(MT):
                last = act.activation(share[:, m, 0:E], logit[:, m, :], ACT.Exp, bias=neg_top[:, m:m + 1])
            last.then_inc(top_exp, 1)

            def copy_gathered(b):
                act.wait_ge(xg_done, b + 1)
                act.activation(xg, bank[:, BX, :], ACT.Identity).then_inc(xg_ready, 1)

            def copy_gatheredT(b):
                act.wait_ge(xgT_done, b + 1)
                act.activation(xgT, bank[:, BX, :], ACT.Identity).then_inc(xgT_ready, 1)

            copy_gathered(0)
            copy_gatheredT(0)

            def expert_block(b):
                act.wait_ge(gate_ready, b + 1)
                act.activation(sig_s, gate_s, ACT.Sigmoid, scale=ALPHA).then_inc(sigm_ready, 1)
                copy_gathered(b + 1)
                act.wait_ge(scatT_done, b + 2)
                act.wait_ge(scatter_done, b + 1)
                act.activation(scatT, bank[:, BU, 0:T], ACT.Identity).then_inc(scatT_ready, 1)
                copy_gatheredT(b + 1)

            act.sem_inc(scatT_ready, 1)
            with act.Fori(0, E) as b:
                expert_block(b)
            act.wait_ge(ctrl_ready, 1)
            n_over = act.value_load(ctrl[0:1, OVER:OVER + 1], min_val=0, max_val=OVER_MAX)
            with act.Fori(0, OVER_MAX) as j:
                with act.If(j < n_over):
                    expert_block(j + E)
                act.nop()
            act.wait_ge(x2_ready, N_OUT + MT)
            square_sum(2, h2[:, 1, :])


_INS = ["x", "norm1_g", "w_in", "b_in", "na_rpb", "swa_sinks", "w_up_a", "w_up_b", "w_out", "norm2_g",
        "w_router", "b_router", "w1", "b1", "w2", "b2", "final_g"]


def kernel(**inputs):
    import concourse.bacc as bacc
    from concourse.bass_utils import run_bass_kernel_spmd

    nc = bacc.Bacc("TRN2", target_bir_lowering=False, num_devices=1)
    arrays, args = {}, []
    for name, a in [("consts", shape_constants())] + [(n, np.ascontiguousarray(inputs[n])) for n in _INS]:
        arrays[f"in_{name}"] = a
        args.append(nc.dram_tensor(f"in_{name}", a.shape, mybir.dt.from_np(a.dtype), kind="ExternalInput").ap())
    out = nc.dram_tensor("out_0", (1, T, D), F32, kind="ExternalOutput").ap()
    build_block(nc, *args, out)
    r = run_bass_kernel_spmd(nc, [arrays], core_ids=[0])
    return r.results[0]["out_0"]
```

```python
from contextlib import ExitStack

import numpy as np

import concourse.bass as bass
from concourse import mybir

F32 = mybir.dt.float32
BF16 = mybir.dt.bfloat16
I32 = mybir.dt.int32
ALU = mybir.AluOpType
ACT = mybir.ActivationFunctionType
AX = mybir.AxisListType

P = 128
D = 1024
T = 256
MT = T // P
KD = D // P
GRID_W, ROWS, NA_ROWS, NA_COLS = 64, 4, 8, 16
HEADS, DH = 8, 64
NA_W = HEADS * DH
KV_HEADS = 2
WINDOW = 128
THETA = 10000.0
E, TOPK, FF = 32, 4, 1024
LIMIT, ALPHA, EPS = 7.0, 1.702, 1e-5
D_IN = 3 * NA_W + NA_W + 2 * KV_HEADS * DH + 2 * D
SCALE = DH ** -0.5

CW = 256
SLOT_F = 2048
SLOTS = 12
N_IN = D_IN // CW
N_UP = 4
N_OUT = D // CW
PRE = N_IN + N_UP + N_OUT
W1_CH, W2_CH = D // P, FF // (2 * P)
CAP = 64
OVER = 16
OVER_MAX = T * TOPK // (CAP + 1)
NBC = E + OVER
DR = 6
RPB_W = 2 * NA_COLS - 1
RPB = (2 * NA_ROWS - 1) * RPB_W
NEG = -1.0e30
FAR = 4096.0

_W = [("ident", P), ("rot", P), ("dup", 2 * P), ("dup_rot", 2 * P), ("cos", T), ("sin", T),
      ("na_mask", GRID_W), ("swa_mask", MT * T), ("before", P), ("slot", P), ("over", OVER), ("expert", 1)]
CONST = {}
_at = 0
for _n, _w in _W:
    CONST[_n] = slice(_at, _at + _w)
    _at += _w
CONST_W = _at


def shape_constants():
    c = np.zeros((P, CONST_W), np.float32)
    half = DH // 2
    i = np.arange(P)
    c[:, CONST["ident"]] = np.eye(P)
    rot = np.zeros((P, P), np.float32)
    for d in range(P):
        if d % DH < half:
            rot[d + half, d] = -1.0
        else:
            rot[d - half, d] = 1.0
    c[:, CONST["rot"]] = rot
    for g in range(KV_HEADS):
        dup = np.zeros((P, P), np.float32)
        dup[g * DH + i % DH, i] = 1.0
        c[:, CONST["dup"]][:, g * P:(g + 1) * P] = dup
        c[:, CONST["dup_rot"]][:, g * P:(g + 1) * P] = rot @ dup
    inv = (THETA ** (-np.arange(half, dtype=np.float32) / half)).astype(np.float32)
    ang = np.arange(T, dtype=np.float32)[None, :] * inv[i % half][:, None]
    c[:, CONST["cos"]] = np.cos(ang)
    c[:, CONST["sin"]] = np.sin(ang)
    col = i % GRID_W
    first = np.clip(col - NA_COLS // 2, 0, GRID_W - NA_COLS)[:, None]
    key = np.arange(GRID_W)[None, :]
    near = np.where((key >= first) & (key < first + NA_COLS), 0.0, NEG)
    c[:, CONST["na_mask"]] = near.reshape(P // GRID_W, GRID_W, GRID_W)[:, ::-1].reshape(P, GRID_W)
    q = np.arange(MT)[None, :, None] * P + i[:, None, None]
    k = np.arange(T)[None, None, :]
    c[:, CONST["swa_mask"]] = np.where(np.abs(k - q) <= WINDOW, 0.0, NEG).reshape(P, MT * T)
    c[:, CONST["before"]] = i[:, None] < i[None, :]
    c[:, CONST["slot"]] = i[None, :] % CAP
    c[:, CONST["over"]] = np.arange(OVER)[None, :]
    c[:, CONST["expert"]] = i[:, None]
    return c


class Chain:

    def __init__(self, eng, sem):
        self.eng, self.sem, self.base, self.n = eng, sem, 0, 0

    def link(self, ins):
        ins.then_inc(self.sem, 1)
        self.n += 1
        self.eng.wait_ge(self.sem, self.base + self.n)


def build_block(nc, consts, x_in, norm1_g, w_in, b_in, na_rpb, swa_sinks, w_up_a, w_up_b, w_out,
                norm2_g, w_router, b_router, w1, b1, w2, b2, final_g, out):
    with ExitStack() as ctx:
        def sb(name, shape, dt=F32):
            return ctx.enter_context(nc.sbuf_tensor(name, shape, dt))

        def sem(name):
            return ctx.enter_context(nc.semaphore(name))

        ring = sb("ring", [P, SLOTS, SLOT_F])
        cst = sb("cst", [P, CONST_W])
        x = sb("x", [P, MT, D])
        hT = sb("hT", [P, KD, T])
        h2 = hT[:].rearrange("p k t -> p (k t)").rearrange("p (m d) -> p m d", m=MT)
        gates = sb("gates", [P, 2 * KD, T])
        h = gates[:, 0:KD, :].rearrange("p k t -> p (k t)").rearrange("p (m d) -> p m d", m=MT)
        merged = gates[:, 0:KD, :]
        x2T = gates[:, KD:2 * KD, :]
        work = sb("work", [P, 4736])
        cut = lambda a, n: work[:, a:a + n]
        qaT = cut(0, 1024).rearrange("p (b t) -> p b t", t=T)
        kaT = cut(1024, 1024).rearrange("p (b t) -> p b t", t=T)
        oT = cut(2048, 2048).rearrange("p (b t) -> p b t", t=T)
        kbT = cut(4096, 512).rearrange("p (g t) -> p g t", t=T)
        xg = cut(0, 512)
        xgT = cut(512, 512)
        gate_s, up_s, sig_s, hid = (cut(1024 + 512 * n, 512) for n in range(4))
        hidT = cut(3072, 512)
        down_s = cut(3584, 512)
        scatT = cut(4096, 256)
        pick = cut(4352, 128).rearrange("p (m s) -> p m s", m=MT)
        pick_g = cut(4480, 256).rearrange("p (m s) -> p m s", m=MT)
        qbT = sb("qbT", [P, 4, T])
        kraw = sb("kraw", [P, T])
        rtmp = sb("rtmp", [P, 2, T])
        rtmp2 = sb("rtmp2", [P, 2, T])
        v_sb = sb("v_sb", [P, MT, NA_W + P])
        v_bias = sb("v_bias", [P, NA_W + P])
        tables = sb("tables", [P, HEADS * DR * GRID_W])
        na_bias = tables[:].rearrange("p (h w) -> p h w", h=HEADS)
        b1_sb = tables[0:E, 0:2 * FF]
        b2_sb = tables[0:E, 2 * FF:2 * FF + D]
        prob = [sb(f"prob{n}", [P, 2, MT, T]) for n in range(2)]
        probT = sb("probT", [P, 2, 2, T])
        vec_rows = sb("vec_rows", [P, P])
        n_vec = D_IN // P + 2 * KD
        vec = sb("vec", [P, n_vec])
        g2_b = sb("g2_b", [P, D])
        gf_b = qbT[:].rearrange("p b t -> p (b t)")
        sink_b = sb("sink_b", [P, HEADS])
        wr = sb("wr", [P, KD, E])
        br_b = sb("br_b", [P, E])
        ones = sb("ones", [P, P])
        zeros = sb("zeros", [1, 512], BF16)
        minus_half = sb("minus_half", [P, MT])
        ssq_part = sb("ssq_part", [P, N_OUT, MT])
        ssq = sb("ssq", [P, 3, MT])
        msq = sb("msq", [P, 3, MT])
        rstd = sb("rstd", [P, 3, MT])
        mx = sb("mx", [P, 2, 2])
        neg_mx = sb("neg_mx", [P, 2, 2])
        den = sb("den", [P, 2, 2])
        e_sink = sb("e_sink", [P, 2, 2])
        logT = kraw[0:E, :]
        logit = sb("logit", [P, MT, E])
        top8 = sb("top8", [P, MT, 8])
        n_gt = sb("n_gt", [P, MT])
        neg_top = sb("neg_top", [P, MT])
        g_sum = sb("g_sum", [P, MT])
        above = sb("above", [P, MT, E])
        equal = sb("equal", [P, MT, E])
        nth = sb("nth", [P, MT, E])
        chosen = sb("chosen", [P, MT, E])
        place = sb("place", [P, MT, NBC])
        share = sb("share", [P, MT, NBC])
        is_exp = sb("is_exp", [E, NBC])
        shareT, placeT = rtmp[0:E, 0, :], rtmp[0:E, 1, :]
        extra = sb("extra", [E, 4])
        from_j = sb("from_j", [E, OVER])
        sel_off = sb("sel_off", [E, OVER])
        ctrl = sb("ctrl", [1, OVER + 1], I32)
        b1_pick = sb("b1_pick", [E, CAP])

        bank = ctx.enter_context(nc.psum_tensor("bank", [P, 8, 512], F32))
        quarter = lambda b: bank[:, b, :].rearrange("p (a t) -> p a t", t=P)
        half_ = lambda b: bank[:, b, :].rearrange("p (a t) -> p a t", t=T)

        rank_done = sem("rank_done")
        x_landed = [sem(f"x_landed{m}") for m in range(MT)]
        ident_landed, consts_landed, vec_landed = sem("ident_landed"), sem("consts_landed"), sem("vec_landed")
        attn_small_landed, bias_landed = sem("attn_small_landed"), sem("bias_landed")
        final_g_landed = sem("final_g_landed")
        route_landed, expert_bias_landed = sem("route_landed"), sem("expert_bias_landed")
        landed = [sem(f"chunk_landed{n}") for n in range(SLOTS)]
        chunk_used = sem("chunk_used")
        dve_step = sem("dve_step")
        pool_step = sem("pool_step")
        ones_set, ssq_act = sem("ones_set"), sem("ssq_act")
        msq_ready, rstd_ready, h_ready = sem("msq_ready"), sem("rstd_ready"), sem("h_ready")
        hT_done, hT_ready = sem("hT_done"), sem("hT_ready")
        vec_done, vec_ready = sem("vec_done"), sem("vec_ready")
        proj_read_dve, proj_read_act = sem("proj_read_dve"), sem("proj_read_act")
        masked_bias, rope_done, rope_ready = sem("masked_bias"), sem("rope_done"), sem("rope_ready")
        scores_done, max_ready, exp_ready = sem("scores_done"), sem("max_ready"), sem("exp_ready")
        prob_ready, probT_done, probT_ready = sem("prob_ready"), sem("probT_done"), sem("probT_ready")
        o_done, o_ready, sig_ready = sem("o_done"), sem("o_ready"), sem("sig_ready")
        merged_ready, x2_ready = sem("merged_ready"), sem("x2_ready")
        h2_ready, x2T_done, x2T_ready = sem("h2_ready"), sem("x2T_done"), sem("x2T_ready")
        logT_done, logT_ready, log_done = sem("logT_done"), sem("logT_ready"), sem("log_done")
        top_ready, top_exp, chosen_ready, count_done = sem("top_ready"), sem("top_exp"), sem("chosen_ready"), sem("count_done")
        place_ready, extra_ready, start_done = sem("place_ready"), sem("extra_ready"), sem("start_done")
        tr_done, tr_ready, list_done, ctrl_ready = sem("tr_done"), sem("tr_ready"), sem("list_done"), sem("ctrl_ready")
        pick_ready, pick_g_ready, b1_pick_ready = sem("pick_ready"), sem("pick_g_ready"), sem("b1_pick_ready")
        xg_done, xg_ready, xgT_done, xgT_ready = sem("xg_done"), sem("xg_ready"), sem("xgT_done"), sem("xgT_ready")
        gate_ready, sigm_ready, hid_ready = sem("gate_ready"), sem("sigm_ready"), sem("hid_ready")
        hidT_done, hidT_ready = sem("hidT_done"), sem("hidT_ready")
        scatT_done, scatT_ready, down_ready, scatter_done = sem("scatT_done"), sem("scatT_ready"), sem("down_ready"), sem("scatter_done")
        y_done, out_ready, out_stored = sem("y_done"), sem("out_ready"), sem("out_stored")

        def C(name):
            return cst[:, CONST[name]]

        def slot_of(chunk):
            return chunk % SLOTS

        def landings(chunk):
            return 16 * (chunk // SLOTS + 1)

        def expert_slot(c):
            return slot_of(PRE + c), landings(PRE + c)

        BLK = W1_CH + W2_CH
        assert BLK == SLOTS and N_IN * CW == D_IN

        UNITS = HEADS
        GATE_C = 9
        ROPE_C = GATE_C
        UNIT_C = [4, 6, 7, 8, 11, 12, 13, 14]
        TURN_C = [6, 7, 8, 9, 12, 13, 14, 15]
        unit_at = lambda table, c: table.index(c) if c in table else None
        LAST_PLAIN = TURN_C[-1]
        BS, BT, BO, BK = 3, 5, 7, 2
        BG, BU, BX, BH = 4, 5, 6, 7

        def from_right(v):
            v = v.rearrange("p (r c) -> p r c", c=GRID_W)
            return bass.AP(v.tensor, v.offset + GRID_W - 1, [list(d) for d in v.ap[:2]] + [[-1, GRID_W]])

        def bcast(v, at, n):
            return bass.AP(v.tensor, at, [[0, P], [1, n]])

        block = ctx.enter_context(nc.Block())

        @block.sync
        def _(sp):
            for m in range(MT):
                sp.dma_start(x[:, m, :], x_in[0, m * P:(m + 1) * P, :]).then_inc(x_landed[m], 16)
            sp.dma_start(C("ident"), consts[:, CONST["ident"]]).then_inc(ident_landed, 16)
            sp.dma_start(vec_rows[0:D_IN // P, :], b_in.rearrange("l (b p) -> (l b) p", p=P)).then_inc(vec_landed, 16)
            for i, g in enumerate((norm1_g, norm2_g)):
                at = D_IN // P + i * KD
                sp.dma_start(vec_rows[at:at + KD, :], g.rearrange("l (b p) -> (l b) p", p=P)).then_inc(vec_landed, 16)

            def chunk_source(n):
                if n < N_IN:
                    return w_in[0, :, n * CW:(n + 1) * CW].rearrange("(k p) n -> p k n", p=P)
                n -= N_IN
                if n < N_UP:
                    w = (w_up_a, w_up_b)[n % 2]
                    return w[0, :, n // 2 * 512:(n // 2 + 1) * 512].rearrange("(k p) n -> p k n", p=P)
                n -= N_UP
                return w_out[0, :, n * CW:(n + 1) * CW].rearrange("(k p) n -> p k n", p=P)

            for n in range(PRE):
                if n >= SLOTS:
                    sp.wait_ge(chunk_used, n - SLOTS + 1)
                src = chunk_source(n)
                dst = ring[:, slot_of(n), :].rearrange("p (k n) -> p k n", n=src.shape[2])
                sp.dma_start(dst, src).then_inc(landed[slot_of(n)], 16)
                if n == 2:
                    sp.dma_start(cst[:, P:], consts[:, P:]).then_inc(consts_landed, 16)
                if n == 3:
                    sp.dma_start(v_bias[:, 0:NA_W], bcast(b_in, 2 * NA_W, NA_W)).then_inc(attn_small_landed, 16)
                    sp.dma_start(v_bias[:, NA_W:], bcast(b_in, 4 * NA_W + P, P)).then_inc(attn_small_landed, 16)
                    sp.dma_start(sink_b[:], bcast(swa_sinks, 0, HEADS)).then_inc(attn_small_landed, 16)
                    for r in range(2):
                        for hd in range(HEADS):
                            at = hd * RPB + (NA_ROWS - 1 - 2 - r) * RPB_W + NA_COLS - 1
                            src = bass.AP(na_rpb.tensor, at - (GRID_W - 1), [[1, GRID_W], [RPB_W, DR], [1, GRID_W]])
                            dst = na_bias[r * GRID_W:(r + 1) * GRID_W, hd, :].rearrange("p (a c) -> p a c", c=GRID_W)
                            sp.dma_start(dst, src).then_inc(bias_landed, 16)
                if n == 8:
                    sp.dma_start(g2_b[:], bcast(norm2_g, 0, D)).then_inc(route_landed, 16)
                    sp.dma_start(wr[:], w_router[0].rearrange("(k p) e -> p k e", p=P)).then_inc(route_landed, 16)
                    sp.dma_start(br_b[:], bcast(b_router, 0, E)).then_inc(route_landed, 16)
                if n == PRE - 2:
                    sp.wait_ge(scores_done, UNITS)
                    sp.dma_start(gf_b, bcast(final_g, 0, D)).then_inc(final_g_landed, 16)
                    sp.dma_start(b1_sb, b1[0]).then_inc(expert_bias_landed, 16)
                    sp.dma_start(b2_sb, b2[0]).then_inc(expert_bias_landed, 16)

            def load_expert(e, blk):
                one = bass.ds(e, 1)
                for c in range(BLK):
                    sp.wait_ge(chunk_used, blk * BLK + PRE + c - SLOTS + 1)
                    s = expert_slot(c)[0]
                    if c < W1_CH:
                        src = w1[0, one, c * P:(c + 1) * P, :].rearrange("e p n -> p (e n)")
                        dst = ring[:, s, :]
                    else:
                        r0 = (c - W1_CH) * 2 * P
                        src = w2[0, one, r0:r0 + 2 * P, :].rearrange("e (j p) n -> p (e j) n", p=P)
                        dst = ring[:, s, :].rearrange("p (j n) -> p j n", j=2)
                    sp.dma_start(dst, src).then_inc(landed[s], 16)

            with sp.Fori(0, E) as blk:
                load_expert(blk, blk)
            sp.wait_ge(ctrl_ready, 1)
            n_over = sp.value_load(ctrl[0:1, OVER:OVER + 1], min_val=0, max_val=OVER_MAX)
            with sp.If(n_over > 0):
                with sp.Fori(0, OVER_MAX) as j:
                    with sp.If(j < n_over):
                        e = sp.value_load(ctrl[0:1, bass.ds(j, 1)], min_val=0, max_val=E - 1)
                        load_expert(e, j + E)
                    sp.nop()
                sp.nop()
            for m in range(MT):
                sp.wait_ge(out_ready, m + 1)
                sp.dma_start(out[0, m * P:(m + 1) * P, :], h2[:, m, :]).then_inc(out_stored, 16)
            sp.wait_ge(out_stored, 16 * MT)

        @block.gpsimd
        def _(pool):
            pool.memset(ones[:], 1.0).then_inc(ones_set, 1)
            pool.memset(zeros[:], 0.0).then_inc(ones_set, 1)
            pool.memset(minus_half[:], -0.5).then_inc(pool_step, 1)
            pool.wait_ge(pool_step, 1)

            def power(n, tiles, count):
                pool.wait_ge(msq_ready, count)
                pool.tensor_tensor(rstd[:, n, tiles], msq[:, n, tiles], minus_half[:, tiles], ALU.pow).then_inc(rstd_ready, 1)

            power(0, slice(0, 1), 1)
            power(0, slice(1, 2), 2)
            pool.wait_ge(bias_landed, 16 * 2 * HEADS)
            pool.wait_ge(consts_landed, 16)
            for hd in range(HEADS):
                v = na_bias[:, hd, :].rearrange("p (a c) -> p a c", c=GRID_W)
                mask = C("na_mask").rearrange("p (o c) -> p o c", o=1).to_broadcast([P, DR, GRID_W])
                pool.tensor_tensor(v, v, mask, ALU.add).then_inc(masked_bias, 1)
            power(1, slice(0, MT), 3)
            power(2, slice(0, 1), 4)
            power(2, slice(1, 2), 5)

        @block.tensor
        def _(pe):
            pe.wait_ge(ident_landed, 16)
            pe.wait_ge(vec_landed, 48)
            pe.transpose(bank[:, 4, 0:n_vec], vec_rows[0:n_vec, :], C("ident")[0:n_vec, 0:n_vec]).then_inc(vec_done, 1)
            for m in range(MT):
                pe.wait_ge(h_ready, m + 1)
                for a in range(2):
                    for j in range(4):
                        k = 4 * a + j
                        last = pe.transpose(quarter(2 * m + a)[:, j, :], h[:, m, k * P:(k + 1) * P], C("ident"))
                    last.then_inc(hT_done, 1)
            pe.wait_ge(hT_ready, 2 * MT)

            def project(c):
                if c >= 3:
                    if c - 3 < GATE_C:
                        pe.wait_ge(proj_read_dve, c - 2)
                    else:
                        pe.wait_ge(proj_read_act, c - 3 - GATE_C + 1)
                if c % 3 == BK and c > ROPE_C:
                    pe.wait_ge(rope_ready, 1)
                w = ring[:, slot_of(c), :].rearrange("p (k n) -> p k n", n=CW)
                pe.wait_ge(landed[slot_of(c)], landings(c))
                dst = half_(c % 3)
                for a in range(2):
                    for k in range(KD):
                        st = dict(start=k == 0, stop=k == KD - 1)
                        if c in (4, 5):
                            last = pe.matmul(dst[:, a, :], hT[:, k, a * P:(a + 1) * P], w[:, k, :], **st)
                        elif c == 8 and a == 1:
                            continue
                        else:
                            last = pe.matmul(dst[:, a, :], w[:, k, a * P:(a + 1) * P], hT[:, k, :], **st)
                if c == 8:
                    for m in range(MT):
                        for k in range(KD):
                            last = pe.matmul(dst[:, 1, m * P:(m + 1) * P], hT[:, k, m * P:(m + 1) * P],
                                             w[:, k, P:2 * P], start=k == 0, stop=k == KD - 1)
                last.then_inc(chunk_used, 1)

            def scores(u):
                pair = u % 4
                if u == 0:
                    pe.wait_ge(proj_read_dve, 4)
                if u == 4:
                    pe.wait_ge(rope_ready, 1)
                if u:
                    pe.wait_ge(max_ready, u)
                for qt in range(MT):
                    for i in range(2):
                        rows = slice(DH * i, DH * i + DH)
                        q, k = (qaT, kaT[:, pair, :]) if u < 4 else (qbT[:], kbT[:, pair // 2, :])
                        last = pe.matmul(bank[:, BS + i, qt * T:(qt + 1) * T], q[rows, pair, qt * P:(qt + 1) * P],
                                         k[rows, :], start=True, stop=True)
                last.then_inc(scores_done, 1)

            def turn_probs(u):
                pe.wait_ge(prob_ready, u + 1)
                if u:
                    pe.wait_ge(probT_ready, u)
                if u == 4:
                    pe.wait_ge(rope_ready, 1)
                for i in range(2):
                    for kt in range(2):
                        for qt in range(MT):
                            last = pe.transpose(bank[:, BT + i, kt * T + qt * P:kt * T + (qt + 1) * P],
                                                prob[u % 2][:, i, qt, kt * P:(kt + 1) * P], C("ident"))
                last.then_inc(probT_done, 1)

            def attend(u):
                pair = u % 4
                pe.wait_ge(probT_ready, u + 1)
                if u == 0:
                    pe.wait_ge(proj_read_dve, 6)
                if u:
                    pe.wait_ge(o_ready, u)
                for kt in range(2):
                    for i in range(2):
                        col = (2 * pair + i) * DH if u < 4 else NA_W + pair // 2 * DH
                        last = pe.matmul(bank[DH * i:DH * i + DH, BO, 0:T], v_sb[:, kt, col:col + DH],
                                         probT[:, i, kt, :], start=kt == 0, stop=kt == 1)
                last.then_inc(o_done, 1)

            def rotate():
                pe.wait_ge(consts_landed, 16)
                pe.wait_ge(proj_read_dve, GATE_C)
                pe.wait_ge(o_ready, 4)
                for b in range(4):
                    pe.matmul(half_(BT + b // 2)[:, b % 2, :], C("rot"), qbT[:, b, :], start=True, stop=True)
                for g in range(KV_HEADS):
                    pe.matmul(half_(BO)[:, g, :], C("dup")[:, g * P:(g + 1) * P], kraw[:], start=True, stop=True)
                    last = pe.matmul(half_(BK)[:, g, :], C("dup_rot")[:, g * P:(g + 1) * P], kraw[:],
                                     start=True, stop=True)
                last.then_inc(rope_done, 1)

            for c in range(N_IN):
                turned, scored = unit_at(TURN_C, c), unit_at(UNIT_C, c)
                if turned is not None:
                    turn_probs(turned)
                if scored is not None:
                    scores(scored)
                if turned is not None:
                    attend(turned)
                project(c)
                if c == ROPE_C:
                    rotate()

            pe.wait_ge(o_ready, UNITS)
            pe.wait_ge(proj_read_act, N_IN - GATE_C)
            for n in range(N_UP):
                c, branch = N_IN + n, n % 2
                w = ring[:, slot_of(c), :].rearrange("p (k n) -> p k n", n=512)
                pe.wait_ge(landed[slot_of(c)], landings(c))
                for j in range(4):
                    for k in range(4):
                        last = pe.matmul(half_(2 * n + j // 2)[:, j % 2, :], w[:, k, j * P:(j + 1) * P],
                                         oT[:, 4 * branch + k, :], start=k == 0, stop=k == 3)
                last.then_inc(chunk_used, 1)

            LOG = 7

            def router(n):
                pe.wait_ge(x2_ready, n + 1)
                dst = half_(4 + n % 2)
                if n >= 2:
                    pe.wait_ge(x2T_ready, n - 1)
                for j in range(2):
                    for m in range(MT):
                        last = pe.transpose(dst[:, j, m * P:(m + 1) * P], x[:, m, n * CW + j * P:n * CW + (j + 1) * P],
                                            C("ident"))
                last.then_inc(x2T_done, 1)

            def router_product(n):
                pe.wait_ge(x2T_ready, n + 1)
                for k in range(2 * n, 2 * n + 2):
                    last = pe.matmul(bank[0:E, LOG, 0:T], wr[:, k, :], x2T[:, k, :], start=k == 0, stop=k == KD - 1)
                if n == N_OUT - 1:
                    last.then_inc(logT_done, 1)

            pe.wait_ge(route_landed, 48)
            for n in range(N_OUT):
                c = N_IN + N_UP + n
                w = ring[:, slot_of(c), :].rearrange("p (k n) -> p k n", n=CW)
                pe.wait_ge(landed[slot_of(c)], landings(c))
                for m in range(MT):
                    for k in range(KD):
                        if k in (0, 4):
                            pe.wait_ge(merged_ready, k // 4 + 1)
                        last = pe.matmul(half_(n)[:, m, :], merged[:, k, m * P:(m + 1) * P], w[:, k, :],
                                         start=k == 0, stop=k == KD - 1)
                last.then_inc(chunk_used, 1)
                if n:
                    router(n - 1)
                if n > 1:
                    router_product(n - 2)
            router_product(N_OUT - 2)
            router(N_OUT - 1)
            router_product(N_OUT - 1)
            pe.wait_ge(logT_ready, 1)
            for m in range(MT):
                last = pe.transpose(bank[:, 6, m * E:(m + 1) * E], logT[:, m * P:(m + 1) * P], C("ident")[0:E, 0:E])
            last.then_inc(log_done, 1)
            pe.wait_ge(chosen_ready, 1)
            pe.wait_ge(ones_set, 2)
            pe.matmul(bank[:, 5, 0:E], C("before"), chosen[:, 0, :], start=True, stop=True)
            pe.matmul(bank[:, 5, E:2 * E], ones[:], chosen[:, 0, :], start=True, stop=False)
            last = pe.matmul(bank[:, 5, E:2 * E], C("before"), chosen[:, 1, :], start=False, stop=True)
            last.then_inc(rank_done, 1)
            for m in range(MT):
                last = pe.matmul(bank[0:E, 7, 0:1], chosen[:, m, :], ones[:, 0:1], start=m == 0, stop=m == 1)
            last.then_inc(count_done, 1)

            def gather():
                for m in range(MT):
                    for a in range(2):
                        last = pe.matmul(bank[CAP * a:CAP * (a + 1), BX, :], pick[:, m, :],
                                         h2[:, m, a * 512:(a + 1) * 512], start=m == 0, stop=m == 1)
                last.then_inc(xg_done, 1)

            def turn(dst, src, n, done):
                for j in range(n):
                    last = pe.transpose(quarter(dst)[:, j, :], src(j), C("ident"))
                last.then_inc(done, 1)

            turn_gathered = lambda: turn(BX, lambda j: xg[:, j * P:(j + 1) * P], 4, xgT_done)

            pe.wait_ge(pick_ready, 1)
            pe.wait_ge(h2_ready, MT)
            gather()
            pe.wait_ge(xg_ready, 1)
            turn_gathered()

            def start_sum():
                for m in range(MT):
                    for a in range(2):
                        pe.matmul(bank[:, 2 * m + a, :], C("ident"), x[:, m, a * 512:(a + 1) * 512],
                                  start=True, stop=False, skip_group_check=True)
                        pe.matmul(bank[:, 2 * m + a, :], shareT[:, m * P:(m + 1) * P], b2_sb[:, a * 512:(a + 1) * 512],
                                  start=False, stop=False, skip_group_check=True)

            def list_blocks():
                pe.wait_ge(extra_ready, 1)
                pe.matmul(bank[0:E, BX, 0:1], C("before")[0:E, 0:E], extra[:, 0:1], start=True, stop=True).then_inc(start_done, 1)
                pe.wait_ge(tr_ready, 1)
                for m in range(MT):
                    pe.transpose(bank[0:E, BH, m * P:(m + 1) * P], share[:, m, 0:E], C("ident"))
                    last = pe.transpose(bank[0:E, BH, (2 + m) * P:(3 + m) * P], place[:, m, 0:E], C("ident"))
                last.then_inc(tr_done, 1)
                pe.wait_ge(tr_ready, 2)
                over = is_exp[:, E:NBC]
                for m in range(MT):
                    tok = slice(m * P, (m + 1) * P)
                    pe.matmul(bank[:, BX, m * OVER:(m + 1) * OVER], placeT[:, tok], over, start=True, stop=False)
                    pe.matmul(bank[:, BX, m * OVER:(m + 1) * OVER], ones[0:E, :], sel_off[:], start=False, stop=True)
                    pe.matmul(bank[:, BX, (2 + m) * OVER:(3 + m) * OVER], shareT[:, tok], over, start=True, stop=True)
                pe.matmul(bank[0:1, BX, 4 * OVER:5 * OVER], C("expert")[0:E, :], over, start=True, stop=True)
                pe.matmul(bank[0:1, BX, 5 * OVER:5 * OVER + 1], extra[:, 0:1], ones[0:E, 0:1],
                          start=True, stop=True).then_inc(list_done, 1)
                start_sum()
                pe.wait_ge(ctrl_ready, 1)

            def expert_block(b, first=False):
                pe.wait_ge(xgT_ready, b + 1)
                pe.wait_ge(b1_pick_ready, b + 1)
                pe.wait_ge(scatT_ready, b + 1)
                parts = [(BG, 0), (BG, 1), (BU, 0), (BU, 1)]
                for q, (bk, a) in enumerate(parts):
                    pe.matmul(bank[CAP * a:CAP * (a + 1), bk, :], b1_pick[:], b1_sb[:, q * 512:(q + 1) * 512],
                              start=True, stop=False)
                for k in range(W1_CH):
                    s, count = expert_slot(k)
                    pe.wait_ge(landed[s], b * 16 + count)
                    kT = xgT[:, (k % 4) * P + k // 4 * CAP:(k % 4) * P + (k // 4 + 1) * CAP]
                    for q, (bk, a) in enumerate(parts):
                        last = pe.matmul(bank[CAP * a:CAP * (a + 1), bk, :], kT, ring[:, s, q * 512:(q + 1) * 512],
                                         start=False, stop=k == W1_CH - 1)
                    last.then_inc(chunk_used, 1)
                if first:
                    list_blocks()
                pe.wait_ge(pick_ready, b + 2)
                gather()
                pe.wait_ge(hid_ready, b + 1)
                turn(BH, lambda j: hid[:, j * P:(j + 1) * P], 4, hidT_done)
                pe.wait_ge(pick_g_ready, b + 1)
                turn(BU, lambda m: pick_g[:, m, :], MT, scatT_done)
                pe.wait_ge(xg_ready, b + 2)
                turn_gathered()
                pe.wait_ge(hidT_ready, b + 1)
                for f in range(2 * W2_CH):
                    s, count = expert_slot(W1_CH + f // 2)
                    if f % 2 == 0:
                        pe.wait_ge(landed[s], b * 16 + count)
                    fT = hidT[:, (f % 4) * P + f // 4 * CAP:(f % 4) * P + (f // 4 + 1) * CAP]
                    for a in range(2):
                        last = pe.matmul(bank[CAP * a:CAP * (a + 1), BH, :], fT,
                                         ring[:, s, f % 2 * D + a * 512:f % 2 * D + (a + 1) * 512],
                                         start=f == 0, stop=f == 2 * W2_CH - 1)
                    if f % 2:
                        last.then_inc(chunk_used, 1)
                pe.wait_ge(down_ready, b + 1)
                pe.wait_ge(scatT_ready, b + 2)
                for m in range(MT):
                    for a in range(2):
                        rows = slice(CAP * a, CAP * (a + 1))
                        last = pe.matmul(bank[:, 2 * m + a, :], scatT[rows, m * P:(m + 1) * P], down_s[rows, :],
                                         start=False, stop=False, skip_group_check=True)
                last.then_inc(scatter_done, 1)

            pe.sem_inc(scatT_done, 1)
            pe.sem_inc(scatter_done, 1)
            pe.wait_ge(expert_bias_landed, 32)
            expert_block(0, first=True)
            with pe.Fori(1, E) as b:
                expert_block(b)
            n_over = pe.value_load(ctrl[0:1, OVER:OVER + 1], min_val=0, max_val=OVER_MAX)
            with pe.If(n_over > 0):
                with pe.Fori(0, OVER_MAX) as j:
                    with pe.If(j < n_over):
                        expert_block(j + E)
                    pe.nop()
                pe.nop()
            for m in range(MT):
                for a in range(2):
                    last = pe.matmul(bank[:, 2 * m + a, :], zeros[0:1, 0:P], zeros[0:1, :],
                                     start=False, stop=True, skip_group_check=True)
                last.then_inc(y_done, 1)

        @block.vector
        def _(dve):
            ch = Chain(dve, dve_step)

            def norm1():
                dve.wait_ge(x_landed[0], 16)
                ch.link(dve.tensor_tensor_reduce(out=h[:, 0, :], in0=x[:, 0, :], in1=x[:, 0, :], scale=1.0, scalar=0.0,
                                                 op0=ALU.mult, op1=ALU.add, accum_out=ssq[:, 0, 0:1]))
                for m in range(MT):
                    if m == 1:
                        dve.wait_ge(ssq_act, 1)
                    dve.tensor_scalar(msq[:, 0, m:m + 1], ssq[:, 0, m:m + 1], 1.0 / D, EPS,
                                      ALU.mult, ALU.add).then_inc(msq_ready, 1)
                    dve.wait_ge(rstd_ready, m + 1)
                    dve.tensor_scalar(h[:, m, :], x[:, m, :], rstd[:, 0, m:m + 1], None, ALU.mult).then_inc(h_ready, 1)

            dve.wait_ge(ones_set, 2)
            norm1()
            dve.wait_ge(vec_done, 1)
            dve.tensor_copy(vec[:], bank[:, 4, 0:n_vec]).then_inc(vec_ready, 1)
            dve.wait_ge(vec_ready, 1)
            for g in range(2 * MT):
                m, a = g // 2, g % 2
                dve.wait_ge(hT_done, g + 1)
                g1 = vec[:, D_IN // P + 4 * a:D_IN // P + 4 * a + 4].rearrange("p (k o) -> p k o", o=1)
                dve.tensor_tensor(hT[:, 4 * a:4 * a + 4, m * P:(m + 1) * P], quarter(g),
                                  g1.to_broadcast([P, 4, P]), ALU.mult).then_inc(hT_ready, 1)

            def read_projection(c):
                dve.wait_ge(chunk_used, c + 1)
                src = half_(c % 3)
                if c in (4, 5):
                    col = slice((c - 4) * CW, (c - 3) * CW)
                    bias = v_bias[:, col].rearrange("p (o n) -> p o n", o=1).to_broadcast([P, MT, CW])
                    last = dve.tensor_tensor(v_sb[:, :, col], src, bias, ALU.add)
                elif c == 8:
                    dve.tensor_scalar(kraw[:], src[:, 0, :], vec[:, 2 * c:2 * c + 1], None, ALU.add)
                    bias = v_bias[:, NA_W:].rearrange("p (o n) -> p o n", o=1).to_broadcast([P, MT, P])
                    last = dve.tensor_tensor(v_sb[:, :, NA_W:], src[:, 1, :].rearrange("p (m n) -> p m n", m=MT),
                                             bias, ALU.add)
                else:
                    for a in range(2):
                        b = 2 * c + a
                        bias = vec[:, b:b + 1]
                        if c < 2:
                            last = dve.tensor_scalar(qaT[:, b, :].rearrange("p (r c) -> p r c", c=GRID_W),
                                                     from_right(src[:, a, :]), bias, SCALE, ALU.add, ALU.mult)
                        elif c < 4:
                            last = dve.tensor_scalar(kaT[:, b - 4, :], src[:, a, :], bias, None, ALU.add)
                        else:
                            last = dve.tensor_scalar(qbT[:, b - 12, :], src[:, a, :], bias, SCALE, ALU.add, ALU.mult)
                last.then_inc(proj_read_dve, 1)

            def rotary():
                two = lambda n: C(n).rearrange("p (o t) -> p o t", o=1).to_broadcast([P, 2, T])
                dve.wait_ge(rope_done, 1)
                for b in range(2):
                    q = qbT[:, 2 * b:2 * b + 2, :]
                    dve.tensor_tensor(rtmp[:], half_(BT + b), two("sin"), ALU.mult)
                    ch.link(dve.tensor_tensor(q, q, two("cos"), ALU.mult))
                    ch.link(dve.tensor_tensor(q, q, rtmp[:], ALU.add))
                dve.tensor_tensor(rtmp[:], half_(BO), two("cos"), ALU.mult)
                ch.link(dve.tensor_tensor(rtmp2[:], half_(BK), two("sin"), ALU.mult))
                dve.tensor_tensor(kbT, rtmp[:], rtmp2[:], ALU.add).then_inc(rope_ready, 1)

            def softmax_front(u):
                pair, s = u % 4, prob[u % 2]
                if u == 0:
                    dve.wait_ge(consts_landed, 16)
                dve.wait_ge(scores_done, u + 1)
                if u >= 2:
                    dve.wait_ge(probT_done, u - 1)
                if u < 4:
                    if u == 0:
                        dve.wait_ge(masked_bias, HEADS)
                    for qt in range(MT):
                        bias = na_bias[:, 2 * pair:2 * pair + 2, (2 - 2 * qt) * GRID_W:(2 - 2 * qt + ROWS) * GRID_W]
                        last = dve.tensor_tensor(s[:, :, qt, :], bank[:, BS:BS + 2, qt * T:(qt + 1) * T], bias, ALU.add)
                else:
                    mask = C("swa_mask").rearrange("p (o t) -> p o t", o=1).to_broadcast([P, 2, MT * T])
                    last = dve.tensor_tensor(s[:].rearrange("p i m t -> p i (m t)"), bank[:, BS:BS + 2, :], mask, ALU.add)
                ch.link(last)
                ch.link(dve.tensor_reduce(mx[:], s[:], AX.X, ALU.max))
                sink = sink_b[:, 2 * pair:2 * pair + 2].rearrange("p (i o) -> p i o", o=1).to_broadcast([P, 2, MT])
                if u >= 4:
                    ch.link(dve.tensor_tensor(mx[:], mx[:], sink, ALU.max))
                    ch.link(dve.tensor_tensor(e_sink[:], sink, mx[:], ALU.subtract))
                dve.tensor_scalar(neg_mx[:], mx[:], -1.0, None, ALU.mult).then_inc(max_ready, 1)

            def softmax_back(u):
                s = prob[u % 2]
                dve.wait_ge(exp_ready, u + 1)
                if u >= 4:
                    ch.link(dve.tensor_tensor(den[:], den[:], e_sink[:], ALU.add))
                ch.link(dve.reciprocal(den[:], den[:]))
                for i in range(2):
                    inv = den[:, i, :].rearrange("p (m o) -> p m o", o=1).to_broadcast([P, MT, T])
                    last = dve.tensor_tensor(s[:, i, :, :], s[:, i, :, :], inv, ALU.mult)
                last.then_inc(prob_ready, 1)

            def read_output(u):
                dve.wait_ge(o_done, u + 1)
                dst, src = oT[:, u, :], bank[:, BO, 0:T]
                if u < 4:
                    dst, src = dst.rearrange("p (r c) -> p r c", c=GRID_W), from_right(src)
                dve.tensor_copy(dst, src).then_inc(o_ready, 1)

            for c in range(N_IN):
                turned, scored = unit_at(TURN_C, c), unit_at(UNIT_C, c)
                if c == 5:
                    dve.wait_ge(attn_small_landed, 48)
                if 1 <= c <= GATE_C:
                    read_projection(c - 1)
                if scored is not None:
                    softmax_front(scored)
                if turned is not None:
                    read_output(turned)
                if scored is not None:
                    softmax_back(scored)
                if c == ROPE_C:
                    rotary()

            dve.wait_ge(sig_ready, 1)
            dve.wait_ge(proj_read_act, N_IN - GATE_C)
            for hf in range(2):
                ga, gb = gates[:, 4 * hf:4 * hf + 4, :], gates[:, KD + 4 * hf:KD + 4 * hf + 4, :]
                lifted = lambda b: bank[:, b:b + 2, :].rearrange("p b (a t) -> p (b a) t", t=T)
                dve.wait_ge(chunk_used, N_IN + 2 * hf + 1)
                dve.tensor_tensor(ga, ga, lifted(4 * hf), ALU.mult)
                dve.wait_ge(chunk_used, N_IN + 2 * hf + 2)
                ch.link(dve.tensor_tensor(gb, gb, lifted(4 * hf + 2), ALU.mult))
                dve.tensor_tensor(ga, ga, gb, ALU.add).then_inc(merged_ready, 1)
            for n in range(N_OUT):
                xs = x[:, :, n * CW:(n + 1) * CW]
                dve.wait_ge(chunk_used, N_IN + N_UP + n + 1)
                dve.tensor_tensor(xs, xs, half_(n), ALU.add).then_inc(x2_ready, 1)
            dve.wait_ge(x2_ready, N_OUT)
            dve.wait_ge(ssq_act, 2)
            ch.link(dve.tensor_reduce(ssq[:, 1, :], ssq_part[:].rearrange("p n m -> p m n"), AX.X, ALU.add))
            dve.tensor_scalar(msq[:, 1, :], ssq[:, 1, :], 1.0 / D, EPS, ALU.mult, ALU.add).then_inc(msq_ready, 1)
            dve.wait_ge(route_landed, 48)
            dve.wait_ge(logT_done, 1)
            dve.tensor_copy(logT, bank[0:E, 7, 0:T]).then_inc(logT_ready, 1)
            dve.wait_ge(rstd_ready, 3)
            dve.wait_ge(log_done, 1)
            for m in range(MT):
                last = dve.scalar_tensor_tensor(out=logit[:, m, :], in0=bank[:, 6, m * E:(m + 1) * E],
                                                scalar=rstd[:, 1, m:m + 1], in1=br_b[:], op0=ALU.mult, op1=ALU.add)
            ch.link(last)
            for m in range(MT):
                last = dve.max(top8[:, m, :], logit[:, m, :])
            ch.link(last)
            dve.tensor_scalar(neg_top[:], top8[:, :, 0], -1.0, None, ALU.mult).then_inc(top_ready, 1)
            fourth = top8[:, :, TOPK - 1:TOPK].to_broadcast([P, MT, E])
            dve.tensor_tensor(equal[:], logit[:], fourth, ALU.is_equal)
            ch.link(dve.tensor_tensor(above[:], logit[:], fourth, ALU.is_gt))
            ch.link(dve.tensor_reduce(n_gt[:], above[:], AX.X, ALU.add))
            for m in range(MT):
                last = dve.tensor_tensor_scan(nth[:, m, :], ones[:, 0:E], equal[:, m, :], n_gt[:, m:m + 1],
                                              ALU.mult, ALU.add)
            ch.link(last)
            ch.link(dve.scalar_tensor_tensor(out=equal[:], in0=nth[:], scalar=float(TOPK), in1=equal[:],
                                             op0=ALU.is_le, op1=ALU.mult))
            dve.tensor_tensor(chosen[:], above[:], equal[:], ALU.add).then_inc(chosen_ready, 1)
            dve.memset(place[:, :, E:NBC], -1.0)
            for m in range(MT):
                dve.scalar_tensor_tensor(out=h2[:, m, :], in0=x[:, m, :], scalar=rstd[:, 1, m:m + 1], in1=g2_b[:],
                                         op0=ALU.mult, op1=ALU.mult).then_inc(h2_ready, 1)
            dve.wait_ge(chosen_ready, 1)
            dve.wait_ge(rank_done, 1)
            rank = bank[:, 5, 0:MT * E].rearrange("p (m e) -> p m e", m=MT)
            ch.link(dve.scalar_tensor_tensor(out=place[:, :, 0:E], in0=rank, scalar=FAR, in1=chosen[:],
                                             op0=ALU.add, op1=ALU.mult))
            dve.tensor_scalar(place[:, :, 0:E], place[:, :, 0:E], -FAR, None, ALU.add).then_inc(place_ready, 1)
            dve.wait_ge(place_ready, 1)

            def make_pick(col):
                for m in range(MT):
                    last = dve.tensor_scalar(pick[:, m, :], C("slot")[:, 0:CAP], place[:, m, col], None, ALU.is_equal)
                last.then_inc(pick_ready, 1)

            def make_b1_pick(col):
                dve.tensor_copy(b1_pick[:], is_exp[:, col].to_broadcast([E, CAP])).then_inc(b1_pick_ready, 1)

            make_pick(bass.ds(0, 1))
            ch.link(dve.tensor_copy(is_exp[:, 0:E], C("ident")[0:E, 0:E]))
            make_b1_pick(bass.ds(0, 1))
            dve.wait_ge(top_exp, 1)
            ch.link(dve.tensor_tensor(share[:, :, 0:E], share[:, :, 0:E], chosen[:], ALU.mult))
            ch.link(dve.tensor_reduce(g_sum[:], share[:, :, 0:E], AX.X, ALU.add))
            ch.link(dve.reciprocal(g_sum[:], g_sum[:]))
            inv = g_sum[:].rearrange("p (m o) -> p m o", o=1).to_broadcast([P, MT, E])
            ch.link(dve.tensor_tensor(share[:, :, 0:E], share[:, :, 0:E], inv, ALU.mult))

            def list_blocks():
                dve.wait_ge(count_done, 1)
                count = bank[0:E, BH, 0:1]
                dve.tensor_scalar(extra[:, 1:2], count, float(CAP), None, ALU.is_gt)
                ch.link(dve.tensor_scalar(extra[:, 2:3], count, float(2 * CAP), None, ALU.is_gt))
                dve.tensor_scalar(extra[:, 3:4], count, float(3 * CAP), None, ALU.is_gt)
                ch.link(dve.tensor_tensor(extra[:, 1:2], extra[:, 1:2], extra[:, 2:3], ALU.add))
                dve.tensor_tensor(extra[:, 0:1], extra[:, 1:2], extra[:, 3:4], ALU.add).then_inc(extra_ready, 1)
                dve.wait_ge(start_done, 1)
                over = is_exp[:, E:NBC]
                ch.link(dve.tensor_copy(extra[:, 1:2], bank[0:E, BX, 0:1]))
                ch.link(dve.tensor_scalar(from_j[:], C("over")[0:E, :], extra[:, 1:2], None, ALU.subtract))
                dve.tensor_scalar(sel_off[:], from_j[:], 0.0, None, ALU.is_ge)
                ch.link(dve.tensor_scalar(over, from_j[:], extra[:, 0:1], None, ALU.is_lt))
                ch.link(dve.tensor_tensor(over, over, sel_off[:], ALU.mult))
                ch.link(dve.tensor_scalar(from_j[:], from_j[:], 1.0, -float(CAP), ALU.add, ALU.mult))
                dve.tensor_tensor(sel_off[:], from_j[:], over, ALU.mult).then_inc(tr_ready, 1)
                dve.wait_ge(tr_done, 1)
                dve.tensor_copy(shareT, bank[0:E, BH, 0:T])
                dve.tensor_copy(placeT, bank[0:E, BH, T:2 * T]).then_inc(tr_ready, 1)
                dve.wait_ge(list_done, 1)
                lists = bank[:, BX, 0:4 * OVER].rearrange("p (a m j) -> p a m j", a=2, m=MT)
                dve.tensor_copy(place[:, :, E:NBC], lists[:, 0])
                dve.tensor_copy(share[:, :, E:NBC], lists[:, 1])
                dve.tensor_copy(ctrl[:], bank[0:1, BX, 4 * OVER:5 * OVER + 1]).then_inc(ctrl_ready, 1)
                dve.wait_ge(ctrl_ready, 1)

            chain = [ch.n]
            STEPS = 2

            def expert_block(b, first=False):
                one, nxt = bass.ds(b, 1), bass.ds(b + 1, 1)
                if first:
                    list_blocks()
                    chain[0] = ch.n
                ch.base, ch.n = b * STEPS + chain[0], 0
                dve.wait_ge(scatT_done, b + 1)
                for m in range(MT):
                    last = dve.tensor_scalar(pick_g[:, m, :], C("slot"), place[:, m, one], share[:, m, one],
                                             ALU.is_equal, ALU.mult)
                last.then_inc(pick_g_ready, 1)
                dve.wait_ge(xg_done, b + 1)
                make_pick(nxt)
                dve.wait_ge(chunk_used, b * BLK + PRE + W1_CH)
                dve.tensor_scalar(gate_s, bank[:, BG, :], LIMIT, None, ALU.min).then_inc(gate_ready, 1)
                ch.link(dve.tensor_scalar(up_s, bank[:, BU, :], LIMIT, -LIMIT, ALU.min, ALU.max))
                dve.wait_ge(gate_ready, b + 1)
                ch.link(dve.scalar_tensor_tensor(out=up_s, in0=up_s, scalar=1.0, in1=gate_s, op0=ALU.add, op1=ALU.mult))
                dve.wait_ge(sigm_ready, b + 1)
                dve.tensor_tensor(hid, up_s, sig_s, ALU.mult).then_inc(hid_ready, 1)
                make_b1_pick(nxt)
                dve.wait_ge(hidT_done, b + 1)
                dve.tensor_copy(hidT, bank[:, BH, :]).then_inc(hidT_ready, 1)
                dve.wait_ge(chunk_used, b * BLK + PRE + BLK)
                dve.wait_ge(scatter_done, b + 1)
                dve.tensor_copy(down_s, bank[:, BH, :]).then_inc(down_ready, 1)
                assert ch.n == STEPS

            expert_block(0, first=True)
            with dve.Fori(1, E) as b:
                expert_block(b)
            n_over = dve.value_load(ctrl[0:1, OVER:OVER + 1], min_val=0, max_val=OVER_MAX)
            with dve.If(n_over > 0):
                with dve.Fori(0, OVER_MAX) as j:
                    with dve.If(j < n_over):
                        expert_block(j + E)
                    dve.nop()
                dve.nop()
            dve.wait_ge(final_g_landed, 16)
            for m in range(MT):
                dve.wait_ge(ssq_act, 3 + m)
                dve.tensor_scalar(msq[:, 2, m:m + 1], ssq[:, 2, m:m + 1], 1.0 / D, EPS,
                                  ALU.mult, ALU.add).then_inc(msq_ready, 1)
                dve.wait_ge(rstd_ready, 4 + m)
                dve.scalar_tensor_tensor(out=h2[:, m, :], in0=bank[:, 2 * m:2 * m + 2, :].rearrange("p b n -> p (b n)"),
                                         scalar=rstd[:, 2, m:m + 1], in1=gf_b, op0=ALU.mult, op1=ALU.mult).then_inc(out_ready, 1)

        @block.scalar
        def _(act):
            act.wait_ge(x_landed[1], 16)
            act.activation(h[:, 1, :], x[:, 1, :], ACT.Square, accum_out=ssq[:, 0, 1:2]).then_inc(ssq_act, 1)
            act.wait_ge(vec_ready, 1)

            def exponentials(u):
                s = prob[u % 2]
                act.wait_ge(max_ready, u + 1)
                if u >= 4:
                    act.activation(e_sink[:], e_sink[:], ACT.Exp)
                for i in range(2):
                    for qt in range(MT):
                        last = act.activation(s[:, i, qt, :], s[:, i, qt, :], ACT.Exp,
                                              bias=neg_mx[:, i, qt:qt + 1], accum_out=den[:, i, qt:qt + 1])
                last.then_inc(exp_ready, 1)

            def read_probs(u):
                act.wait_ge(probT_done, u + 1)
                if u:
                    act.wait_ge(o_done, u)
                act.activation(probT[:].rearrange("p i k t -> p (i k t)"),
                               bank[:, BT:BT + 2, :].rearrange("p b n -> p (b n)"), ACT.Identity).then_inc(probT_ready, 1)

            def read_gates(c):
                act.wait_ge(chunk_used, c + 1)
                for a in range(2):
                    b = 2 * (c - GATE_C) + a
                    last = act.activation(gates[:, b, :], half_(c % 3)[:, a, :],
                                          ACT.Identity if c < LAST_PLAIN else ACT.Sigmoid, bias=vec[:, 2 * c + a:2 * c + a + 1])
                last.then_inc(proj_read_act, 1)

            for c in range(N_IN + 1):
                turned, scored = unit_at(TURN_C, c), unit_at(UNIT_C, c)
                if turned is not None:
                    read_probs(turned)
                if c > GATE_C:
                    read_gates(c - 1)
                if scored is not None:
                    exponentials(scored)
                if c == LAST_PLAIN:
                    act.wait_ge(proj_read_act, c - GATE_C)
                    n = 2 * (c - GATE_C)
                    act.activation(gates[:, 0:n, :], gates[:, 0:n, :], ACT.Sigmoid).then_inc(sig_ready, 1)
            g2 = D_IN // P + KD
            for n in range(N_OUT):
                act.wait_ge(x2_ready, n + 1)
                for m in range(MT):
                    last = act.activation(h2[:, m, n * CW:(n + 1) * CW], x[:, m, n * CW:(n + 1) * CW], ACT.Square,
                                          accum_out=ssq_part[:, n, m:m + 1])
                if n == N_OUT - 1:
                    last.then_inc(ssq_act, 1)
                act.wait_ge(x2T_done, n + 1)
                for j in range(2):
                    k = 2 * n + j
                    last = act.activation(x2T[:, k, :], half_(4 + n % 2)[:, j, :], ACT.Identity,
                                          scale=vec[:, g2 + k:g2 + k + 1])
                last.then_inc(x2T_ready, 1)
            act.wait_ge(top_ready, 1)
            for m in range(MT):
                last = act.activation(share[:, m, 0:E], logit[:, m, :], ACT.Exp, bias=neg_top[:, m:m + 1])
            last.then_inc(top_exp, 1)

            def copy_gathered(b):
                act.wait_ge(xg_done, b + 1)
                act.activation(xg, bank[:, BX, :], ACT.Identity).then_inc(xg_ready, 1)

            def copy_gatheredT(b):
                act.wait_ge(xgT_done, b + 1)
                act.activation(xgT, bank[:, BX, :], ACT.Identity).then_inc(xgT_ready, 1)

            copy_gathered(0)
            copy_gatheredT(0)

            def expert_block(b):
                act.wait_ge(gate_ready, b + 1)
                act.activation(sig_s, gate_s, ACT.Sigmoid, scale=ALPHA).then_inc(sigm_ready, 1)
                copy_gathered(b + 1)
                act.wait_ge(scatT_done, b + 2)
                act.wait_ge(scatter_done, b + 1)
                act.activation(scatT, bank[:, BU, 0:T], ACT.Identity).then_inc(scatT_ready, 1)
                copy_gatheredT(b + 1)

            act.sem_inc(scatT_ready, 1)
            expert_block(0)
            with act.Fori(1, E) as b:
                expert_block(b)
            act.wait_ge(ctrl_ready, 1)
            n_over = act.value_load(ctrl[0:1, OVER:OVER + 1], min_val=0, max_val=OVER_MAX)
            with act.If(n_over > 0):
                with act.Fori(0, OVER_MAX) as j:
                    with act.If(j < n_over):
                        expert_block(j + E)
                    act.nop()
                act.nop()
            for m in range(MT):
                act.wait_ge(y_done, m + 1)
                act.activation(x[:, m, :], bank[:, 2 * m:2 * m + 2, :].rearrange("p b n -> p (b n)"), ACT.Square,
                               accum_out=ssq[:, 2, m:m + 1]).then_inc(ssq_act, 1)


_INS = ["x", "norm1_g", "w_in", "b_in", "na_rpb", "swa_sinks", "w_up_a", "w_up_b", "w_out", "norm2_g",
        "w_router", "b_router", "w1", "b1", "w2", "b2", "final_g"]


def kernel(**inputs):
    import concourse.bacc as bacc
    from concourse.bass_utils import run_bass_kernel_spmd

    nc = bacc.Bacc("TRN2", target_bir_lowering=False, num_devices=1)
    arrays, args = {}, []
    for name, a in [("consts", shape_constants())] + [(n, np.ascontiguousarray(inputs[n])) for n in _INS]:
        arrays[f"in_{name}"] = a
        args.append(nc.dram_tensor(f"in_{name}", a.shape, mybir.dt.from_np(a.dtype), kind="ExternalInput").ap())
    out = nc.dram_tensor("out_0", (1, T, D), F32, kind="ExternalOutput").ap()
    build_block(nc, *args, out)
    r = run_bass_kernel_spmd(nc, [arrays], core_ids=[0])
    return r.results[0]["out_0"]
```

```python
from contextlib import ExitStack

import numpy as np

import concourse.bass as bass
from concourse import mybir

F32 = mybir.dt.float32
BF16 = mybir.dt.bfloat16
I32 = mybir.dt.int32
ALU = mybir.AluOpType
ACT = mybir.ActivationFunctionType
AX = mybir.AxisListType

P = 128
D = 1024
T = 256
MT = T // P
KD = D // P
GRID_W, ROWS, NA_ROWS, NA_COLS = 64, 4, 8, 16
HEADS, DH = 8, 64
NA_W = HEADS * DH
KV_HEADS = 2
WINDOW = 128
THETA = 10000.0
E, TOPK, FF = 32, 4, 1024
LIMIT, ALPHA, EPS = 7.0, 1.702, 1e-5
D_IN = 3 * NA_W + NA_W + 2 * KV_HEADS * DH + 2 * D
SCALE = DH ** -0.5

CW = 256
SLOT_F = 2048
SLOTS = 12
N_IN = D_IN // CW
N_UP = 4
N_OUT = D // CW
PRE = N_IN + N_UP + N_OUT
W1_CH, W2_CH = D // P, FF // (2 * P)
HELD = 10
HELD_EARLY = 6
CAP = 64
PARTS = 3
OVER = 16
OVER_MAX = T * TOPK // (CAP + 1)
NBC = E + OVER
DR = 6
RPB_W = 2 * NA_COLS - 1
RPB = (2 * NA_ROWS - 1) * RPB_W
NEG = -1.0e30
FAR = 4096.0

_W_KEPT = [("ident", P), ("before", P), ("slot", P), ("over", OVER), ("expert", 1), ("groups", PARTS * E)]
_W_ATTN = [("rot", P), ("dup", 2 * P), ("dup_rot", 2 * P), ("cos", T), ("sin", T), ("na_mask", GRID_W),
           ("swa_mask", MT * T)]
KEPT_W, ATTN_W = (sum(w for _, w in part) for part in (_W_KEPT, _W_ATTN))
CONST = {}
_at = 0
for _n, _w in _W_KEPT + _W_ATTN:
    CONST[_n] = slice(_at, _at + _w)
    _at += _w
CONST_W = _at


def shape_constants():
    c = np.zeros((P, CONST_W), np.float32)
    half = DH // 2
    i = np.arange(P)
    c[:, CONST["ident"]] = np.eye(P)
    rot = np.zeros((P, P), np.float32)
    for d in range(P):
        if d % DH < half:
            rot[d + half, d] = -1.0
        else:
            rot[d - half, d] = 1.0
    c[:, CONST["rot"]] = rot
    for g in range(KV_HEADS):
        dup = np.zeros((P, P), np.float32)
        dup[g * DH + i % DH, i] = 1.0
        c[:, CONST["dup"]][:, g * P:(g + 1) * P] = dup
        c[:, CONST["dup_rot"]][:, g * P:(g + 1) * P] = rot @ dup
    inv = (THETA ** (-np.arange(half, dtype=np.float32) / half)).astype(np.float32)
    ang = np.arange(T, dtype=np.float32)[None, :] * inv[i % half][:, None]
    c[:, CONST["cos"]] = np.cos(ang)
    c[:, CONST["sin"]] = np.sin(ang)
    col = i % GRID_W
    first = np.clip(col - NA_COLS // 2, 0, GRID_W - NA_COLS)[:, None]
    key = np.arange(GRID_W)[None, :]
    near = np.where((key >= first) & (key < first + NA_COLS), 0.0, NEG)
    c[:, CONST["na_mask"]] = near.reshape(P // GRID_W, GRID_W, GRID_W)[:, ::-1].reshape(P, GRID_W)
    q = np.arange(MT)[None, :, None] * P + i[:, None, None]
    k = np.arange(T)[None, None, :]
    c[:, CONST["swa_mask"]] = np.where(np.abs(k - q) <= WINDOW, 0.0, NEG).reshape(P, MT * T)
    c[:, CONST["before"]] = i[:, None] < i[None, :]
    c[:, CONST["slot"]] = i[None, :] % CAP
    c[:, CONST["over"]] = np.arange(OVER)[None, :]
    c[:, CONST["expert"]] = i[:, None]
    c[:, CONST["groups"]] = i[:, None] == np.arange(PARTS * E)[None, :] % E
    return c


class Chain:

    def __init__(self, eng, sem):
        self.eng, self.sem, self.base, self.n = eng, sem, 0, 0

    def link(self, ins):
        ins.then_inc(self.sem, 1)
        self.n += 1
        self.eng.wait_ge(self.sem, self.base + self.n)


def build_block(nc, consts, x_in, norm1_g, w_in, b_in, na_rpb, swa_sinks, w_up_a, w_up_b, w_out,
                norm2_g, w_router, b_router, w1, b1, w2, b2, final_g, out):
    with ExitStack() as ctx:
        def sb(name, shape, dt=F32):
            return ctx.enter_context(nc.sbuf_tensor(name, shape, dt))

        def sem(name):
            return ctx.enter_context(nc.semaphore(name))

        ring = sb("ring", [P, SLOTS, SLOT_F])
        cst = sb("cst", [P, KEPT_W])
        hT = sb("hT", [P, KD, T])
        h2 = hT[:].rearrange("p k t -> p (k t)").rearrange("p (m d) -> p m d", m=MT)
        held = sb("held", [P, HELD, SLOT_F])
        arena = held[:].rearrange("p s n -> p (s n)")
        left, right = [0], [HELD * SLOT_F]

        def attn_buf(n):
            left[0] += n
            return arena[:, left[0] - n:left[0]]

        def late_buf(n):
            right[0] -= n
            return arena[:, right[0]:right[0] + n]

        x = late_buf(MT * D).rearrange("p (m d) -> p m d", m=MT)
        g2_b = late_buf(D)
        UNTIL_NORM2 = 2
        wr = late_buf(KD * E).rearrange("p (k e) -> p k e", e=E)
        gates = late_buf(2 * KD * T).rearrange("p (k t) -> p k t", t=T)
        h = gates[:, 0:KD, :].rearrange("p k t -> p (k t)").rearrange("p (m d) -> p m d", m=MT)
        merged = gates[:, 0:KD, :]
        x2T = gates[:, KD:2 * KD, :]
        work = sb("work", [P, 4224])
        cut = lambda a, n: work[:, a:a + n]
        qaT = cut(0, 1024).rearrange("p (b t) -> p b t", t=T)
        kaT = cut(1024, 1024).rearrange("p (b t) -> p b t", t=T)
        oT = cut(2048, 2048).rearrange("p (b t) -> p b t", t=T)
        xg = cut(0, 512)
        xgT = cut(512, 512)
        gate_s, up_s, sig_s = (cut(1024 + 512 * n, 512) for n in range(3))
        hid = up_s
        hidT = cut(2560, 512)
        down_s = cut(3072, 512)
        scatT = cut(3584, 256)
        pick = cut(3840, 128).rearrange("p (m s) -> p m s", m=MT)
        pick_g = cut(3968, 256).rearrange("p (m s) -> p m s", m=MT)
        qbT = attn_buf(4 * T).rearrange("p (b t) -> p b t", t=T)
        kbT = attn_buf(2 * T).rearrange("p (g t) -> p g t", t=T)
        attn_cst = attn_buf(ATTN_W)
        kraw = sb("kraw", [P, T])
        rtmp = sb("rtmp", [P, 2, T])
        rtmp2 = attn_buf(2 * T).rearrange("p (g t) -> p g t", t=T)
        v_sb = attn_buf(MT * (NA_W + P)).rearrange("p (m n) -> p m n", m=MT)
        v_bias = attn_buf(NA_W + P)
        tables = sb("tables", [P, HEADS * DR * GRID_W])
        na_bias = tables[:].rearrange("p (h w) -> p h w", h=HEADS)
        b1_raw = tables[0:PARTS * E, 0:2 * FF]
        b1_parts = tables[0:PARTS * E, 2 * FF:3 * FF].bitcast(BF16)
        b2_sb = tables[0:E, 0:D]
        prob = [attn_buf(2 * MT * T).rearrange("p (i m t) -> p i m t", m=MT, t=T) for n in range(2)]
        probT = attn_buf(4 * T).rearrange("p (i k t) -> p i k t", k=2, t=T)
        vec_rows = attn_buf(P)
        assert left[0] <= right[0] and HELD_EARLY * SLOT_F <= right[0]
        n_vec = D_IN // P + 2 * KD
        vec = sb("vec", [P, n_vec])
        gf_b = held[:, 0, 0:D]
        sink_b = sb("sink_b", [P, HEADS])
        br_b = sb("br_b", [P, E])
        ones = sb("ones", [P, P])
        minus_half = sb("minus_half", [P, MT])
        ssq_part = sb("ssq_part", [P, N_OUT, MT])
        ssq = sb("ssq", [P, 3, MT])
        msq = sb("msq", [P, 3, MT])
        rstd = sb("rstd", [P, 3, MT])
        mx = sb("mx", [P, 2, 2])
        neg_mx = sb("neg_mx", [P, 2, 2])
        den = sb("den", [P, 2, 2])
        e_sink = sb("e_sink", [P, 2, 2])
        logT = kraw[0:E, :]
        logit = sb("logit", [P, MT, E])
        top8 = sb("top8", [P, MT, 8])
        n_gt = sb("n_gt", [P, MT])
        neg_top = sb("neg_top", [P, MT])
        g_sum = sb("g_sum", [P, MT])
        above = sb("above", [P, MT, E])
        equal = sb("equal", [P, MT, E])
        nth = sb("nth", [P, MT, E])
        chosen = sb("chosen", [P, MT, E])
        place = sb("place", [P, MT, NBC])
        share = sb("share", [P, MT, NBC])
        is_exp = sb("is_exp", [PARTS * E, NBC])
        shareT, placeT = rtmp[0:E, 0, :], rtmp[0:E, 1, :]
        extra = sb("extra", [E, 4])
        from_j = sb("from_j", [E, OVER])
        sel_off = sb("sel_off", [E, OVER])
        over = sb("over", [E, OVER])
        ctrl = sb("ctrl", [1, OVER + 1], I32)
        b1_pick = sb("b1_pick", [PARTS * E, CAP], BF16)

        bank = ctx.enter_context(nc.psum_tensor("bank", [P, 8, 512], F32))
        quarter = lambda b: bank[:, b, :].rearrange("p (a t) -> p a t", t=P)
        half_ = lambda b: bank[:, b, :].rearrange("p (a t) -> p a t", t=T)

        rank_done = sem("rank_done")
        x_landed = [sem(f"x_landed{m}") for m in range(MT)]
        ident_landed, consts_landed, vec_landed = sem("ident_landed"), sem("consts_landed"), sem("vec_landed")
        kept_consts_landed, held_landed = sem("kept_consts_landed"), sem("held_landed")
        attn_small_landed, bias_landed = sem("attn_small_landed"), sem("bias_landed")
        final_g_landed = sem("final_g_landed")
        route_landed, b1_landed, b2_landed = sem("route_landed"), sem("b1_landed"), sem("b2_landed")
        b1_split = sem("b1_split")
        landed = [sem(f"chunk_landed{n}") for n in range(SLOTS)]
        chunk_used = sem("chunk_used")
        dve_step = sem("dve_step")
        pool_step = sem("pool_step")
        ones_set, ssq_act = sem("ones_set"), sem("ssq_act")
        msq_ready, rstd_ready, h_ready = sem("msq_ready"), sem("rstd_ready"), sem("h_ready")
        hT_done, hT_ready = sem("hT_done"), sem("hT_ready")
        vec_done, vec_ready = sem("vec_done"), sem("vec_ready")
        proj_read_dve, proj_read_act = sem("proj_read_dve"), sem("proj_read_act")
        masked_bias, rope_done, rope_ready = sem("masked_bias"), sem("rope_done"), sem("rope_ready")
        scores_done, max_ready, exp_ready = sem("scores_done"), sem("max_ready"), sem("exp_ready")
        prob_ready, probT_done, probT_ready = sem("prob_ready"), sem("probT_done"), sem("probT_ready")
        o_done, o_ready, sig_ready = sem("o_done"), sem("o_ready"), sem("sig_ready")
        merged_ready, x2_ready = sem("merged_ready"), sem("x2_ready")
        h2_ready, x2T_done, x2T_ready = sem("h2_ready"), sem("x2T_done"), sem("x2T_ready")
        logT_done, logT_ready, log_done = sem("logT_done"), sem("logT_ready"), sem("log_done")
        top_ready, top_exp, chosen_ready, count_done = sem("top_ready"), sem("top_exp"), sem("chosen_ready"), sem("count_done")
        place_ready, extra_ready, start_done = sem("place_ready"), sem("extra_ready"), sem("start_done")
        tr_done, tr_ready, list_done, ctrl_ready = sem("tr_done"), sem("tr_ready"), sem("list_done"), sem("ctrl_ready")
        pick_ready, pick_g_ready, b1_pick_ready = sem("pick_ready"), sem("pick_g_ready"), sem("b1_pick_ready")
        xg_done, xg_ready, xgT_done, xgT_ready = sem("xg_done"), sem("xg_ready"), sem("xgT_done"), sem("xgT_ready")
        gate_ready, sigm_ready, hid_ready = sem("gate_ready"), sem("sigm_ready"), sem("hid_ready")
        hidT_done, hidT_ready = sem("hidT_done"), sem("hidT_ready")
        scatT_done, scatT_ready, down_ready, scatter_done = sem("scatT_done"), sem("scatT_ready"), sem("down_ready"), sem("scatter_done")
        sum_started = sem("sum_started")
        y_done, out_ready, out_stored = sem("y_done"), sem("out_ready"), sem("out_stored")

        def C(name):
            at = CONST[name]
            if at.start < KEPT_W:
                return cst[:, at]
            return attn_cst[:, at.start - KEPT_W:at.stop - KEPT_W]

        def slot_of(chunk):
            return chunk % SLOTS

        def landings(chunk):
            return 16 * (chunk // SLOTS + 1)

        def expert_slot(c):
            return slot_of(PRE + c), landings(PRE + c)

        BLK = W1_CH + W2_CH
        assert BLK == SLOTS and N_IN * CW == D_IN

        UNITS = HEADS
        GATE_C = 9
        ROPE_C = GATE_C
        UNIT_C = [4, 6, 7, 8, 11, 12, 13, 14]
        TURN_C = [6, 7, 8, 9, 12, 13, 14, 15]
        unit_at = lambda table, c: table.index(c) if c in table else None
        LAST_PLAIN = TURN_C[-1]
        BS, BT, BO, BK = 3, 5, 7, 2
        BG, BU, BX, BH = 4, 5, 6, 7

        def from_right(v):
            v = v.rearrange("p (r c) -> p r c", c=GRID_W)
            return bass.AP(v.tensor, v.offset + GRID_W - 1, [list(d) for d in v.ap[:2]] + [[-1, GRID_W]])

        def bcast(v, at, n):
            return bass.AP(v.tensor, at, [[0, P], [1, n]])

        block = ctx.enter_context(nc.Block())

        @block.sync
        def _(sp):
            for m in range(MT):
                sp.dma_start(x[:, m, :], x_in[0, m * P:(m + 1) * P, :]).then_inc(x_landed[m], 16)
            sp.dma_start(C("ident"), consts[:, CONST["ident"]]).then_inc(ident_landed, 16)
            sp.dma_start(vec_rows[0:D_IN // P, :], b_in.rearrange("l (b p) -> (l b) p", p=P)).then_inc(vec_landed, 16)
            for i, g in enumerate((norm1_g, norm2_g)):
                at = D_IN // P + i * KD
                sp.dma_start(vec_rows[at:at + KD, :], g.rearrange("l (b p) -> (l b) p", p=P)).then_inc(vec_landed, 16)

            def chunk_source(n):
                if n < N_IN:
                    return w_in[0, :, n * CW:(n + 1) * CW].rearrange("(k p) n -> p k n", p=P)
                n -= N_IN
                if n < N_UP:
                    w = (w_up_a, w_up_b)[n % 2]
                    return w[0, :, n // 2 * 512:(n // 2 + 1) * 512].rearrange("(k p) n -> p k n", p=P)
                n -= N_UP
                return w_out[0, :, n * CW:(n + 1) * CW].rearrange("(k p) n -> p k n", p=P)

            for n in range(PRE):
                if n >= SLOTS:
                    sp.wait_ge(chunk_used, n - SLOTS + 1)
                src = chunk_source(n)
                dst = ring[:, slot_of(n), :].rearrange("p (k n) -> p k n", n=src.shape[2])
                sp.dma_start(dst, src).then_inc(landed[slot_of(n)], 16)
                if n == 2:
                    sp.dma_start(attn_cst, consts[:, KEPT_W:]).then_inc(consts_landed, 16)
                    sp.dma_start(cst[:, P:], consts[:, P:KEPT_W]).then_inc(kept_consts_landed, 16)
                if n == 3:
                    sp.dma_start(v_bias[:, 0:NA_W], bcast(b_in, 2 * NA_W, NA_W)).then_inc(attn_small_landed, 16)
                    sp.dma_start(v_bias[:, NA_W:], bcast(b_in, 4 * NA_W + P, P)).then_inc(attn_small_landed, 16)
                    sp.dma_start(sink_b[:], bcast(swa_sinks, 0, HEADS)).then_inc(attn_small_landed, 16)
                    for r in range(2):
                        for hd in range(HEADS):
                            at = hd * RPB + (NA_ROWS - 1 - 2 - r) * RPB_W + NA_COLS - 1
                            src = bass.AP(na_rpb.tensor, at - (GRID_W - 1), [[1, GRID_W], [RPB_W, DR], [1, GRID_W]])
                            dst = na_bias[r * GRID_W:(r + 1) * GRID_W, hd, :].rearrange("p (a c) -> p a c", c=GRID_W)
                            sp.dma_start(dst, src).then_inc(bias_landed, 16)
                if n == 8:
                    sp.dma_start(g2_b, bcast(norm2_g, 0, D)).then_inc(route_landed, 16)
                    sp.dma_start(wr[:], w_router[0].rearrange("(k p) e -> p k e", p=P)).then_inc(route_landed, 16)
                    sp.dma_start(br_b[:], bcast(b_router, 0, E)).then_inc(route_landed, 16)
                if n == PRE - 2:
                    sp.wait_ge(scores_done, UNITS)
                    for part in range(PARTS):
                        sp.dma_start(b1_raw[part * E:(part + 1) * E, :], b1[0]).then_inc(b1_landed, 16)

            def chunk_of_w2(e, c, dst):
                r0 = (c - W1_CH) * 2 * P
                src = w2[0, bass.ds(e, 1), r0:r0 + 2 * P, :].rearrange("e (j p) n -> p (e j) n", p=P)
                return sp.dma_start(dst.rearrange("p (j n) -> p j n", j=2), src)

            def load_held(first, last):
                for n in range(first, last):
                    chunk_of_w2(E - HELD + n, BLK - 1, held[:, n, :]).then_inc(held_landed, 16)

            def load_expert(e, blk, has_held=False):
                one = bass.ds(e, 1)
                for c in range(BLK - 1 if has_held else BLK):
                    sp.wait_ge(chunk_used, blk * BLK + PRE + c - SLOTS + 1)
                    s = expert_slot(c)[0]
                    if c < W1_CH:
                        src = w1[0, one, c * P:(c + 1) * P, :].rearrange("e p n -> p (e n)")
                        sp.dma_start(ring[:, s, :], src).then_inc(landed[s], 16)
                    else:
                        chunk_of_w2(e, c, ring[:, s, :]).then_inc(landed[s], 16)

            sp.wait_ge(o_ready, UNITS)
            load_held(0, HELD_EARLY)
            load_expert(0, 0)
            sp.wait_ge(b1_split, 1)
            sp.dma_start(b2_sb, b2[0]).then_inc(b2_landed, 16)
            sp.wait_ge(logT_done, 1)
            load_held(HELD_EARLY, HELD - UNTIL_NORM2)
            sp.wait_ge(h2_ready, MT)
            sp.wait_ge(sum_started, 1)
            load_held(HELD - UNTIL_NORM2, HELD)
            with sp.Fori(1, E - HELD) as blk:
                load_expert(blk, blk)
            with sp.Fori(E - HELD, E) as blk:
                load_expert(blk, blk, has_held=True)
            sp.wait_ge(chunk_used, PRE + (E - HELD + 1) * BLK)
            sp.dma_start(gf_b, bcast(final_g, 0, D)).then_inc(final_g_landed, 16)
            sp.wait_ge(ctrl_ready, 1)
            n_over = sp.value_load(ctrl[0:1, OVER:OVER + 1], min_val=0, max_val=OVER_MAX)
            with sp.If(n_over > 0):
                with sp.Fori(0, OVER_MAX) as j:
                    with sp.If(j < n_over):
                        e = sp.value_load(ctrl[0:1, bass.ds(j, 1)], min_val=0, max_val=E - 1)
                        load_expert(e, j + E)
                    sp.nop()
                sp.nop()
            for m in range(MT):
                for a in range(2):
                    sp.wait_ge(out_ready, 2 * m + a + 1)
                    sp.dma_start(out[0, m * P:(m + 1) * P, a * 512:(a + 1) * 512],
                                 h2[:, m, a * 512:(a + 1) * 512]).then_inc(out_stored, 16)
            sp.wait_ge(out_stored, 2 * 16 * MT)

        @block.gpsimd
        def _(pool):
            pool.memset(ones[:], 1.0).then_inc(ones_set, 1)
            pool.memset(minus_half[:], -0.5).then_inc(pool_step, 1)
            pool.wait_ge(pool_step, 1)

            def power(n, tiles, count):
                pool.wait_ge(msq_ready, count)
                pool.tensor_tensor(rstd[:, n, tiles], msq[:, n, tiles], minus_half[:, tiles], ALU.pow).then_inc(rstd_ready, 1)

            power(0, slice(0, 1), 1)
            power(0, slice(1, 2), 2)
            pool.wait_ge(bias_landed, 16 * 2 * HEADS)
            pool.wait_ge(consts_landed, 16)
            for hd in range(HEADS):
                v = na_bias[:, hd, :].rearrange("p (a c) -> p a c", c=GRID_W)
                mask = C("na_mask").rearrange("p (o c) -> p o c", o=1).to_broadcast([P, DR, GRID_W])
                pool.tensor_tensor(v, v, mask, ALU.add).then_inc(masked_bias, 1)
            power(1, slice(0, MT), 3)
            pool.wait_ge(route_landed, 48)
            pool.wait_ge(rstd_ready, 3)
            pool.tensor_tensor(h2[:, 1, :], x[:, 1, :], g2_b, ALU.mult).then_inc(pool_step, 1)
            pool.wait_ge(pool_step, 2)
            pool.tensor_scalar(h2[:, 1, :], h2[:, 1, :], rstd[:, 1, 1:2], None, ALU.mult).then_inc(h2_ready, 1)
            power(2, slice(0, 1), 4)
            power(2, slice(1, 2), 5)

        @block.tensor
        def _(pe):
            pe.wait_ge(ident_landed, 16)
            pe.wait_ge(vec_landed, 48)
            pe.transpose(bank[:, 4, 0:n_vec], vec_rows[0:n_vec, :], C("ident")[0:n_vec, 0:n_vec]).then_inc(vec_done, 1)
            for m in range(MT):
                pe.wait_ge(h_ready, m + 1)
                for a in range(2):
                    for j in range(4):
                        k = 4 * a + j
                        last = pe.transpose(quarter(2 * m + a)[:, j, :], h[:, m, k * P:(k + 1) * P], C("ident"))
                    last.then_inc(hT_done, 1)
            pe.wait_ge(hT_ready, 2 * MT)

            def project(c):
                if c >= 3:
                    if c - 3 < GATE_C:
                        pe.wait_ge(proj_read_dve, c - 2)
                    else:
                        pe.wait_ge(proj_read_act, c - 3 - GATE_C + 1)
                if c % 3 == BK and c > ROPE_C:
                    pe.wait_ge(rope_ready, 1)
                w = ring[:, slot_of(c), :].rearrange("p (k n) -> p k n", n=CW)
                pe.wait_ge(landed[slot_of(c)], landings(c))
                dst = half_(c % 3)
                for a in range(2):
                    for k in range(KD):
                        st = dict(start=k == 0, stop=k == KD - 1)
                        if c in (4, 5):
                            last = pe.matmul(dst[:, a, :], hT[:, k, a * P:(a + 1) * P], w[:, k, :], **st)
                        elif c == 8 and a == 1:
                            continue
                        else:
                            last = pe.matmul(dst[:, a, :], w[:, k, a * P:(a + 1) * P], hT[:, k, :], **st)
                if c == 8:
                    for m in range(MT):
                        for k in range(KD):
                            last = pe.matmul(dst[:, 1, m * P:(m + 1) * P], hT[:, k, m * P:(m + 1) * P],
                                             w[:, k, P:2 * P], start=k == 0, stop=k == KD - 1)
                last.then_inc(chunk_used, 1)

            def scores(u):
                pair = u % 4
                if u == 0:
                    pe.wait_ge(proj_read_dve, 4)
                if u == 4:
                    pe.wait_ge(rope_ready, 1)
                if u:
                    pe.wait_ge(max_ready, u)
                for qt in range(MT):
                    for i in range(2):
                        rows = slice(DH * i, DH * i + DH)
                        q, k = (qaT, kaT[:, pair, :]) if u < 4 else (qbT[:], kbT[:, pair // 2, :])
                        last = pe.matmul(bank[:, BS + i, qt * T:(qt + 1) * T], q[rows, pair, qt * P:(qt + 1) * P],
                                         k[rows, :], start=True, stop=True)
                last.then_inc(scores_done, 1)

            def turn_probs(u):
                pe.wait_ge(prob_ready, u + 1)
                if u:
                    pe.wait_ge(probT_ready, u)
                if u == 4:
                    pe.wait_ge(rope_ready, 1)
                for i in range(2):
                    for kt in range(2):
                        for qt in range(MT):
                            last = pe.transpose(bank[:, BT + i, kt * T + qt * P:kt * T + (qt + 1) * P],
                                                prob[u % 2][:, i, qt, kt * P:(kt + 1) * P], C("ident"))
                last.then_inc(probT_done, 1)

            def attend(u):
                pair = u % 4
                pe.wait_ge(probT_ready, u + 1)
                if u == 0:
                    pe.wait_ge(proj_read_dve, 6)
                if u:
                    pe.wait_ge(o_ready, u)
                for kt in range(2):
                    for i in range(2):
                        col = (2 * pair + i) * DH if u < 4 else NA_W + pair // 2 * DH
                        last = pe.matmul(bank[DH * i:DH * i + DH, BO, 0:T], v_sb[:, kt, col:col + DH],
                                         probT[:, i, kt, :], start=kt == 0, stop=kt == 1)
                last.then_inc(o_done, 1)

            def rotate():
                pe.wait_ge(consts_landed, 16)
                pe.wait_ge(proj_read_dve, GATE_C)
                pe.wait_ge(o_ready, 4)
                for b in range(4):
                    pe.matmul(half_(BT + b // 2)[:, b % 2, :], C("rot"), qbT[:, b, :], start=True, stop=True)
                for g in range(KV_HEADS):
                    pe.matmul(half_(BO)[:, g, :], C("dup")[:, g * P:(g + 1) * P], kraw[:], start=True, stop=True)
                    last = pe.matmul(half_(BK)[:, g, :], C("dup_rot")[:, g * P:(g + 1) * P], kraw[:],
                                     start=True, stop=True)
                last.then_inc(rope_done, 1)

            for c in range(N_IN):
                turned, scored = unit_at(TURN_C, c), unit_at(UNIT_C, c)
                if turned is not None:
                    turn_probs(turned)
                if scored is not None:
                    scores(scored)
                if turned is not None:
                    attend(turned)
                project(c)
                if c == ROPE_C:
                    rotate()

            pe.wait_ge(o_ready, UNITS)
            pe.wait_ge(proj_read_act, N_IN - GATE_C)
            for n in range(N_UP):
                c, branch = N_IN + n, n % 2
                w = ring[:, slot_of(c), :].rearrange("p (k n) -> p k n", n=512)
                pe.wait_ge(landed[slot_of(c)], landings(c))
                for j in range(4):
                    for k in range(4):
                        last = pe.matmul(half_(2 * n + j // 2)[:, j % 2, :], w[:, k, j * P:(j + 1) * P],
                                         oT[:, 4 * branch + k, :], start=k == 0, stop=k == 3)
                last.then_inc(chunk_used, 1)

            LOG = 7

            def router(n):
                pe.wait_ge(x2_ready, n + 1)
                dst = half_(4 + n % 2)
                if n >= 2:
                    pe.wait_ge(x2T_ready, n - 1)
                for j in range(2):
                    for m in range(MT):
                        last = pe.transpose(dst[:, j, m * P:(m + 1) * P], x[:, m, n * CW + j * P:n * CW + (j + 1) * P],
                                            C("ident"))
                last.then_inc(x2T_done, 1)

            def router_product(n):
                pe.wait_ge(x2T_ready, n + 1)
                for k in range(2 * n, 2 * n + 2):
                    last = pe.matmul(bank[0:E, LOG, 0:T], wr[:, k, :], x2T[:, k, :], start=k == 0, stop=k == KD - 1)
                if n == N_OUT - 1:
                    last.then_inc(logT_done, 1)

            pe.wait_ge(route_landed, 48)
            for n in range(N_OUT):
                c = N_IN + N_UP + n
                w = ring[:, slot_of(c), :].rearrange("p (k n) -> p k n", n=CW)
                pe.wait_ge(landed[slot_of(c)], landings(c))
                for m in range(MT):
                    for k in range(KD):
                        if k in (0, 4):
                            pe.wait_ge(merged_ready, k // 4 + 1)
                        last = pe.matmul(half_(n)[:, m, :], merged[:, k, m * P:(m + 1) * P], w[:, k, :],
                                         start=k == 0, stop=k == KD - 1)
                last.then_inc(chunk_used, 1)
                if n:
                    router(n - 1)
                if n > 1:
                    router_product(n - 2)
            router(N_OUT - 1)
            router_product(N_OUT - 2)
            router_product(N_OUT - 1)

            def start_sum(m):
                for a in range(2):
                    last = pe.matmul(bank[:, 2 * m + a, :], C("ident"), x[:, m, a * 512:(a + 1) * 512],
                                     start=True, stop=False, skip_group_check=True)
                return last

            pe.wait_ge(logT_ready, 1)
            for m in range(MT):
                last = pe.transpose(bank[:, 6, m * E:(m + 1) * E], logT[:, m * P:(m + 1) * P], C("ident")[0:E, 0:E])
            last.then_inc(log_done, 1)
            start_sum(0)
            pe.wait_ge(chosen_ready, 1)
            pe.wait_ge(ones_set, 1)
            pe.wait_ge(kept_consts_landed, 16)
            pe.matmul(bank[:, 5, 0:E], C("before"), chosen[:, 0, :], start=True, stop=True)
            pe.matmul(bank[:, 5, E:2 * E], ones[:], chosen[:, 0, :], start=True, stop=False)
            last = pe.matmul(bank[:, 5, E:2 * E], C("before"), chosen[:, 1, :], start=False, stop=True)
            last.then_inc(rank_done, 1)
            for m in range(MT):
                last = pe.matmul(bank[0:E, 7, 0:1], chosen[:, m, :], ones[:, 0:1],
                                 start=m == 0, stop=m == 1)
            last.then_inc(count_done, 1)
            start_sum(1).then_inc(sum_started, 1)

            def gather():
                for m in range(MT):
                    for a in range(2):
                        last = pe.matmul(bank[CAP * a:CAP * (a + 1), BX, :], pick[:, m, :],
                                         h2[:, m, a * 512:(a + 1) * 512], start=m == 0, stop=m == 1)
                last.then_inc(xg_done, 1)

            def turn(dst, src, n, done):
                for j in range(n):
                    last = pe.transpose(quarter(dst)[:, j, :], src(j), C("ident"))
                last.then_inc(done, 1)

            turn_gathered = lambda: turn(BX, lambda j: xg[:, j * P:(j + 1) * P], 4, xgT_done)


            def add_b2():
                for m in range(MT):
                    for a in range(2):
                        pe.matmul(bank[:, 2 * m + a, :], shareT[:, m * P:(m + 1) * P], b2_sb[:, a * 512:(a + 1) * 512],
                                  start=False, stop=False, skip_group_check=True)

            def list_blocks(step):
                if step == 0:
                    pe.wait_ge(extra_ready, 1)
                    pe.matmul(bank[0:E, BH, 0:1], C("before")[0:E, 0:E], extra[:, 0:1],
                              start=True, stop=True).then_inc(start_done, 1)
                if step == 1:
                    pe.wait_ge(tr_ready, 1)
                    for m in range(MT):
                        pe.transpose(bank[0:E, BH, m * P:(m + 1) * P], share[:, m, 0:E], C("ident"))
                        last = pe.transpose(bank[0:E, BH, (2 + m) * P:(3 + m) * P], place[:, m, 0:E], C("ident"))
                    last.then_inc(tr_done, 1)
                if step == 2:
                    pe.wait_ge(tr_ready, 2)
                    for m in range(MT):
                        tok = slice(m * P, (m + 1) * P)
                        pe.matmul(bank[:, BH, m * OVER:(m + 1) * OVER], placeT[:, tok], over[:], start=True, stop=False)
                        pe.matmul(bank[:, BH, m * OVER:(m + 1) * OVER], ones[0:E, :], sel_off[:], start=False, stop=True)
                        pe.matmul(bank[:, BH, (2 + m) * OVER:(3 + m) * OVER], shareT[:, tok], over[:], start=True, stop=True)
                    pe.matmul(bank[0:PARTS * E, BH, 6 * OVER:7 * OVER], C("groups")[0:E, :], over[:], start=True, stop=True)
                    pe.matmul(bank[0:1, BH, 4 * OVER:5 * OVER], C("expert")[0:E, :], over[:], start=True, stop=True)
                    pe.matmul(bank[0:1, BH, 5 * OVER:5 * OVER + 1], extra[:, 0:1], ones[0:E, 0:1],
                              start=True, stop=True).then_inc(list_done, 1)

            def scatter(closes=False):
                for m in range(MT):
                    for a in range(2):
                        rows = slice(CAP * a, CAP * (a + 1))
                        last = pe.matmul(bank[:, 2 * m + a, :], scatT[rows, m * P:(m + 1) * P], down_s[rows, :],
                                         start=False, stop=closes, skip_group_check=True)
                    if closes:
                        last.then_inc(y_done, 1)
                if not closes:
                    last.then_inc(scatter_done, 1)

            parts = [(BG, 0), (BG, 1), (BU, 0), (BU, 1)]

            LIST_K = [0, 2, 4]

            def add_b1(b):
                pe.wait_ge(b1_pick_ready, b + 1)
                pe.wait_ge(scatT_ready, b + 1)
                for q, (bk, a) in enumerate(parts):
                    pe.matmul(bank[CAP * a:CAP * (a + 1), bk, :], b1_pick[:], b1_parts[:, q * 512:(q + 1) * 512],
                              start=True, stop=False)

            def expert_block(b, first=False):
                if not first:
                    add_b1(b)
                    pe.wait_ge(down_ready, b)
                    pe.wait_ge(scatT_ready, b + 1)
                    scatter()
                pe.wait_ge(xgT_ready, b + 1)
                for k in range(W1_CH):
                    s, count = expert_slot(k)
                    pe.wait_ge(landed[s], b * 16 + count)
                    kT = xgT[:, (k % 4) * P + k // 4 * CAP:(k % 4) * P + (k // 4 + 1) * CAP]
                    for q, (bk, a) in enumerate(parts):
                        last = pe.matmul(bank[CAP * a:CAP * (a + 1), bk, :], kT, ring[:, s, q * 512:(q + 1) * 512],
                                         start=False, stop=k == W1_CH - 1)
                    last.then_inc(chunk_used, 1)
                    if first and k in LIST_K:
                        list_blocks(LIST_K.index(k))
                pe.wait_ge(pick_ready, b + 2)
                gather()
                pe.wait_ge(hid_ready, b + 1)
                turn(BH, lambda j: hid[:, j * P:(j + 1) * P], 4, hidT_done)
                pe.wait_ge(pick_g_ready, b + 1)
                turn(BU, lambda m: pick_g[:, m, :], MT, scatT_done)
                pe.wait_ge(xg_ready, b + 2)
                turn_gathered()
                pe.wait_ge(hidT_ready, b + 1)
                for f in range(2 * W2_CH):
                    s, count = expert_slot(W1_CH + f // 2)
                    if f % 2 == 0:
                        pe.wait_ge(landed[s], b * 16 + count)
                    fT = hidT[:, (f % 4) * P + f // 4 * CAP:(f % 4) * P + (f // 4 + 1) * CAP]
                    for a in range(2):
                        last = pe.matmul(bank[CAP * a:CAP * (a + 1), BH, :], fT,
                                         ring[:, s, f % 2 * D + a * 512:f % 2 * D + (a + 1) * 512],
                                         start=f == 0, stop=f == 2 * W2_CH - 1)
                    if f % 2:
                        last.then_inc(chunk_used, 1)
                if first:
                    pe.wait_ge(b2_landed, 16)
                    add_b2()

            def add_b2():
                for m in range(MT):
                    for a in range(2):
                        pe.matmul(bank[:, 2 * m + a, :], shareT[:, m * P:(m + 1) * P], b2_sb[:, a * 512:(a + 1) * 512],
                                  start=False, stop=False, skip_group_check=True)

            pe.sem_inc(scatT_done, 1)
            pe.sem_inc(scatter_done, 1)
            pe.wait_ge(pick_ready, 1)
            pe.wait_ge(h2_ready, MT)
            gather()
            pe.wait_ge(b1_split, 1)
            add_b1(0)
            pe.wait_ge(xg_ready, 1)
            turn_gathered()
            expert_block(0, first=True)
            with pe.Fori(1, E) as b:
                expert_block(b)
            n_over = pe.value_load(ctrl[0:1, OVER:OVER + 1], min_val=0, max_val=OVER_MAX)
            with pe.If(n_over > 0):
                with pe.Fori(0, OVER_MAX) as j:
                    with pe.If(j < n_over):
                        expert_block(j + E)
                    pe.nop()
                pe.nop()
            pe.wait_ge(down_ready, n_over + E)
            pe.wait_ge(scatT_ready, n_over + (E + 1))
            scatter(closes=True)

        @block.vector
        def _(dve):
            ch = Chain(dve, dve_step)

            def norm1():
                dve.wait_ge(x_landed[0], 16)
                ch.link(dve.tensor_tensor_reduce(out=h[:, 0, :], in0=x[:, 0, :], in1=x[:, 0, :], scale=1.0, scalar=0.0,
                                                 op0=ALU.mult, op1=ALU.add, accum_out=ssq[:, 0, 0:1]))
                for m in range(MT):
                    if m == 1:
                        dve.wait_ge(ssq_act, 1)
                    dve.tensor_scalar(msq[:, 0, m:m + 1], ssq[:, 0, m:m + 1], 1.0 / D, EPS,
                                      ALU.mult, ALU.add).then_inc(msq_ready, 1)
                    dve.wait_ge(rstd_ready, m + 1)
                    dve.tensor_scalar(h[:, m, :], x[:, m, :], rstd[:, 0, m:m + 1], None, ALU.mult).then_inc(h_ready, 1)

            dve.wait_ge(ones_set, 1)
            norm1()
            dve.wait_ge(vec_done, 1)
            dve.tensor_copy(vec[:], bank[:, 4, 0:n_vec]).then_inc(vec_ready, 1)
            dve.wait_ge(vec_ready, 1)
            for g in range(2 * MT):
                m, a = g // 2, g % 2
                dve.wait_ge(hT_done, g + 1)
                g1 = vec[:, D_IN // P + 4 * a:D_IN // P + 4 * a + 4].rearrange("p (k o) -> p k o", o=1)
                dve.tensor_tensor(hT[:, 4 * a:4 * a + 4, m * P:(m + 1) * P], quarter(g),
                                  g1.to_broadcast([P, 4, P]), ALU.mult).then_inc(hT_ready, 1)

            def read_projection(c):
                dve.wait_ge(chunk_used, c + 1)
                src = half_(c % 3)
                if c in (4, 5):
                    col = slice((c - 4) * CW, (c - 3) * CW)
                    bias = v_bias[:, col].rearrange("p (o n) -> p o n", o=1).to_broadcast([P, MT, CW])
                    last = dve.tensor_tensor(v_sb[:, :, col], src, bias, ALU.add)
                elif c == 8:
                    dve.tensor_scalar(kraw[:], src[:, 0, :], vec[:, 2 * c:2 * c + 1], None, ALU.add)
                    bias = v_bias[:, NA_W:].rearrange("p (o n) -> p o n", o=1).to_broadcast([P, MT, P])
                    last = dve.tensor_tensor(v_sb[:, :, NA_W:], src[:, 1, :].rearrange("p (m n) -> p m n", m=MT),
                                             bias, ALU.add)
                else:
                    for a in range(2):
                        b = 2 * c + a
                        bias = vec[:, b:b + 1]
                        if c < 2:
                            last = dve.tensor_scalar(qaT[:, b, :].rearrange("p (r c) -> p r c", c=GRID_W),
                                                     from_right(src[:, a, :]), bias, SCALE, ALU.add, ALU.mult)
                        elif c < 4:
                            last = dve.tensor_scalar(kaT[:, b - 4, :], src[:, a, :], bias, None, ALU.add)
                        else:
                            last = dve.tensor_scalar(qbT[:, b - 12, :], src[:, a, :], bias, SCALE, ALU.add, ALU.mult)
                last.then_inc(proj_read_dve, 1)

            def rotary():
                two = lambda n: C(n).rearrange("p (o t) -> p o t", o=1).to_broadcast([P, 2, T])
                dve.wait_ge(rope_done, 1)
                for b in range(2):
                    q = qbT[:, 2 * b:2 * b + 2, :]
                    dve.tensor_tensor(rtmp[:], half_(BT + b), two("sin"), ALU.mult)
                    ch.link(dve.tensor_tensor(q, q, two("cos"), ALU.mult))
                    ch.link(dve.tensor_tensor(q, q, rtmp[:], ALU.add))
                dve.tensor_tensor(rtmp[:], half_(BO), two("cos"), ALU.mult)
                ch.link(dve.tensor_tensor(rtmp2[:], half_(BK), two("sin"), ALU.mult))
                dve.tensor_tensor(kbT, rtmp[:], rtmp2[:], ALU.add).then_inc(rope_ready, 1)

            def softmax_front(u):
                pair, s = u % 4, prob[u % 2]
                if u == 0:
                    dve.wait_ge(consts_landed, 16)
                dve.wait_ge(scores_done, u + 1)
                if u >= 2:
                    dve.wait_ge(probT_done, u - 1)
                if u < 4:
                    if u == 0:
                        dve.wait_ge(masked_bias, HEADS)
                    for qt in range(MT):
                        bias = na_bias[:, 2 * pair:2 * pair + 2, (2 - 2 * qt) * GRID_W:(2 - 2 * qt + ROWS) * GRID_W]
                        last = dve.tensor_tensor(s[:, :, qt, :], bank[:, BS:BS + 2, qt * T:(qt + 1) * T], bias, ALU.add)
                else:
                    mask = C("swa_mask").rearrange("p (o t) -> p o t", o=1).to_broadcast([P, 2, MT * T])
                    last = dve.tensor_tensor(s[:].rearrange("p i m t -> p i (m t)"), bank[:, BS:BS + 2, :], mask, ALU.add)
                ch.link(last)
                ch.link(dve.tensor_reduce(mx[:], s[:], AX.X, ALU.max))
                sink = sink_b[:, 2 * pair:2 * pair + 2].rearrange("p (i o) -> p i o", o=1).to_broadcast([P, 2, MT])
                if u >= 4:
                    ch.link(dve.tensor_tensor(mx[:], mx[:], sink, ALU.max))
                    ch.link(dve.tensor_tensor(e_sink[:], sink, mx[:], ALU.subtract))
                dve.tensor_scalar(neg_mx[:], mx[:], -1.0, None, ALU.mult).then_inc(max_ready, 1)

            def softmax_back(u):
                s = prob[u % 2]
                dve.wait_ge(exp_ready, u + 1)
                if u >= 4:
                    ch.link(dve.tensor_tensor(den[:], den[:], e_sink[:], ALU.add))
                ch.link(dve.reciprocal(den[:], den[:]))
                for i in range(2):
                    inv = den[:, i, :].rearrange("p (m o) -> p m o", o=1).to_broadcast([P, MT, T])
                    last = dve.tensor_tensor(s[:, i, :, :], s[:, i, :, :], inv, ALU.mult)
                last.then_inc(prob_ready, 1)

            def read_output(u):
                dve.wait_ge(o_done, u + 1)
                dst, src = oT[:, u, :], bank[:, BO, 0:T]
                if u < 4:
                    dst, src = dst.rearrange("p (r c) -> p r c", c=GRID_W), from_right(src)
                dve.tensor_copy(dst, src).then_inc(o_ready, 1)

            for c in range(N_IN):
                turned, scored = unit_at(TURN_C, c), unit_at(UNIT_C, c)
                if c == 5:
                    dve.wait_ge(attn_small_landed, 48)
                if 1 <= c <= GATE_C:
                    read_projection(c - 1)
                if scored is not None:
                    softmax_front(scored)
                if turned is not None:
                    read_output(turned)
                if scored is not None:
                    softmax_back(scored)
                if c == ROPE_C:
                    rotary()

            dve.wait_ge(b1_landed, 16 * PARTS)
            mid, low = slice(E, 2 * E), slice(2 * E, 3 * E)
            ch.link(dve.tensor_copy(b1_parts, b1_raw))
            ch.link(dve.tensor_tensor(b1_raw, b1_raw, b1_parts, ALU.subtract))
            dve.tensor_copy(b1_parts[mid, :], b1_raw[mid, :])
            ch.link(dve.tensor_copy(b1_parts[low, :], b1_raw[low, :]))
            ch.link(dve.tensor_tensor(b1_raw[low, :], b1_raw[low, :], b1_parts[low, :], ALU.subtract))
            dve.tensor_copy(b1_parts[low, :], b1_raw[low, :]).then_inc(b1_split, 1)

            dve.wait_ge(sig_ready, 1)
            dve.wait_ge(proj_read_act, N_IN - GATE_C)
            for hf in range(2):
                ga, gb = gates[:, 4 * hf:4 * hf + 4, :], gates[:, KD + 4 * hf:KD + 4 * hf + 4, :]
                lifted = lambda b: bank[:, b:b + 2, :].rearrange("p b (a t) -> p (b a) t", t=T)
                dve.wait_ge(chunk_used, N_IN + 2 * hf + 1)
                dve.tensor_tensor(ga, ga, lifted(4 * hf), ALU.mult)
                dve.wait_ge(chunk_used, N_IN + 2 * hf + 2)
                ch.link(dve.tensor_tensor(gb, gb, lifted(4 * hf + 2), ALU.mult))
                dve.tensor_tensor(ga, ga, gb, ALU.add).then_inc(merged_ready, 1)
            for n in range(N_OUT):
                xs = x[:, :, n * CW:(n + 1) * CW]
                dve.wait_ge(chunk_used, N_IN + N_UP + n + 1)
                dve.tensor_tensor(xs, xs, half_(n), ALU.add).then_inc(x2_ready, 1)
            dve.wait_ge(x2T_done, N_OUT)
            dve.wait_ge(x2T_ready, N_OUT - 1)
            for k in range(KD - 2, KD):
                g2 = D_IN // P + KD + k
                last = dve.tensor_scalar(x2T[:, k, :], half_(4 + (N_OUT - 1) % 2)[:, k % 2, :], vec[:, g2:g2 + 1], None, ALU.mult)
            last.then_inc(x2T_ready, 1)
            dve.wait_ge(ssq_act, 2)
            ch.link(dve.tensor_reduce(ssq[:, 1, :], ssq_part[:].rearrange("p n m -> p m n"), AX.X, ALU.add))
            dve.tensor_scalar(msq[:, 1, :], ssq[:, 1, :], 1.0 / D, EPS, ALU.mult, ALU.add).then_inc(msq_ready, 1)
            dve.wait_ge(route_landed, 48)
            dve.wait_ge(logT_done, 1)
            dve.tensor_copy(logT, bank[0:E, 7, 0:T]).then_inc(logT_ready, 1)
            dve.wait_ge(rstd_ready, 3)
            dve.wait_ge(log_done, 1)
            for m in range(MT):
                last = dve.scalar_tensor_tensor(out=logit[:, m, :], in0=bank[:, 6, m * E:(m + 1) * E],
                                                scalar=rstd[:, 1, m:m + 1], in1=br_b[:], op0=ALU.mult, op1=ALU.add)
            ch.link(last)
            for m in range(MT):
                last = dve.max(top8[:, m, :], logit[:, m, :])
            ch.link(last)
            dve.tensor_scalar(neg_top[:], top8[:, :, 0], -1.0, None, ALU.mult).then_inc(top_ready, 1)
            fourth = top8[:, :, TOPK - 1:TOPK].to_broadcast([P, MT, E])
            dve.tensor_tensor(equal[:], logit[:], fourth, ALU.is_equal)
            ch.link(dve.tensor_tensor(above[:], logit[:], fourth, ALU.is_gt))
            ch.link(dve.tensor_reduce(n_gt[:], above[:], AX.X, ALU.add))
            for m in range(MT):
                last = dve.tensor_tensor_scan(nth[:, m, :], ones[:, 0:E], equal[:, m, :], n_gt[:, m:m + 1],
                                              ALU.mult, ALU.add)
            ch.link(last)
            ch.link(dve.scalar_tensor_tensor(out=equal[:], in0=nth[:], scalar=float(TOPK), in1=equal[:],
                                             op0=ALU.is_le, op1=ALU.mult))
            dve.tensor_tensor(chosen[:], above[:], equal[:], ALU.add).then_inc(chosen_ready, 1)
            dve.scalar_tensor_tensor(out=h2[:, 0, :], in0=x[:, 0, :], scalar=rstd[:, 1, 0:1], in1=g2_b,
                                     op0=ALU.mult, op1=ALU.mult).then_inc(h2_ready, 1)
            dve.memset(place[:, :, E:NBC], -1.0)
            dve.wait_ge(chosen_ready, 1)
            dve.wait_ge(rank_done, 1)
            rank = bank[:, 5, 0:MT * E].rearrange("p (m e) -> p m e", m=MT)
            ch.link(dve.scalar_tensor_tensor(out=place[:, :, 0:E], in0=rank, scalar=FAR, in1=chosen[:],
                                             op0=ALU.add, op1=ALU.mult))
            dve.tensor_scalar(place[:, :, 0:E], place[:, :, 0:E], -FAR, None, ALU.add).then_inc(place_ready, 1)
            dve.wait_ge(place_ready, 1)
            dve.wait_ge(kept_consts_landed, 16)

            def make_pick(col):
                for m in range(MT):
                    last = dve.tensor_scalar(pick[:, m, :], C("slot")[:, 0:CAP], place[:, m, col], None, ALU.is_equal)
                last.then_inc(pick_ready, 1)

            def make_b1_pick(col):
                dve.tensor_copy(b1_pick[:], is_exp[:, col].to_broadcast([PARTS * E, CAP])).then_inc(b1_pick_ready, 1)

            make_pick(bass.ds(0, 1))
            for part in range(PARTS):
                rows = slice(part * E, (part + 1) * E)
                last = dve.tensor_copy(is_exp[rows, 0:E], C("ident")[rows, rows])
            ch.link(last)
            make_b1_pick(bass.ds(0, 1))
            dve.wait_ge(top_exp, 1)
            ch.link(dve.tensor_tensor(share[:, :, 0:E], share[:, :, 0:E], chosen[:], ALU.mult))
            ch.link(dve.tensor_reduce(g_sum[:], share[:, :, 0:E], AX.X, ALU.add))
            ch.link(dve.reciprocal(g_sum[:], g_sum[:]))
            inv = g_sum[:].rearrange("p (m o) -> p m o", o=1).to_broadcast([P, MT, E])
            ch.link(dve.tensor_tensor(share[:, :, 0:E], share[:, :, 0:E], inv, ALU.mult))

            def count_blocks():
                dve.wait_ge(count_done, 1)
                count = bank[0:E, BH, 0:1]
                dve.tensor_scalar(extra[:, 1:2], count, float(CAP), None, ALU.is_gt)
                ch.link(dve.tensor_scalar(extra[:, 2:3], count, float(2 * CAP), None, ALU.is_gt))
                dve.tensor_scalar(extra[:, 3:4], count, float(3 * CAP), None, ALU.is_gt)
                ch.link(dve.tensor_tensor(extra[:, 1:2], extra[:, 1:2], extra[:, 2:3], ALU.add))
                dve.tensor_tensor(extra[:, 0:1], extra[:, 1:2], extra[:, 3:4], ALU.add).then_inc(extra_ready, 1)

            def list_blocks():
                dve.wait_ge(start_done, 1)
                ch.link(dve.tensor_copy(extra[:, 1:2], bank[0:E, BH, 0:1]))
                ch.link(dve.tensor_scalar(from_j[:], C("over")[0:E, :], extra[:, 1:2], None, ALU.subtract))
                dve.tensor_scalar(sel_off[:], from_j[:], 0.0, None, ALU.is_ge)
                ch.link(dve.tensor_scalar(over[:], from_j[:], extra[:, 0:1], None, ALU.is_lt))
                ch.link(dve.tensor_tensor(over[:], over[:], sel_off[:], ALU.mult))
                ch.link(dve.tensor_scalar(from_j[:], from_j[:], 1.0, -float(CAP), ALU.add, ALU.mult))
                dve.tensor_tensor(sel_off[:], from_j[:], over[:], ALU.mult).then_inc(tr_ready, 1)
                dve.wait_ge(tr_done, 1)
                dve.tensor_copy(shareT, bank[0:E, BH, 0:T])
                dve.tensor_copy(placeT, bank[0:E, BH, T:2 * T]).then_inc(tr_ready, 1)
                dve.wait_ge(list_done, 1)
                lists = bank[:, BH, 0:4 * OVER].rearrange("p (a m j) -> p a m j", a=2, m=MT)
                dve.tensor_copy(place[:, :, E:NBC], lists[:, 0])
                dve.tensor_copy(share[:, :, E:NBC], lists[:, 1])
                dve.tensor_copy(is_exp[:, E:NBC], bank[0:PARTS * E, BH, 6 * OVER:7 * OVER])
                dve.tensor_copy(ctrl[:], bank[0:1, BH, 4 * OVER:5 * OVER + 1]).then_inc(ctrl_ready, 1)
                dve.wait_ge(ctrl_ready, 1)

            chain = [ch.n]
            STEPS = 2

            def expert_block(b, first=False):
                one, nxt = bass.ds(b, 1), bass.ds(b + 1, 1)
                dve.wait_ge(scatT_done, b + 1)
                for m in range(MT):
                    last = dve.tensor_scalar(pick_g[:, m, :], C("slot"), place[:, m, one], share[:, m, one],
                                             ALU.is_equal, ALU.mult)
                last.then_inc(pick_g_ready, 1)
                dve.wait_ge(xg_done, b + 1)
                make_pick(nxt)
                if first:
                    count_blocks()
                    list_blocks()
                    chain[0] = ch.n
                ch.base, ch.n = b * STEPS + chain[0], 0
                dve.wait_ge(chunk_used, b * BLK + PRE + W1_CH)
                dve.tensor_scalar(gate_s, bank[:, BG, :], LIMIT, None, ALU.min).then_inc(gate_ready, 1)
                ch.link(dve.tensor_scalar(up_s, bank[:, BU, :], LIMIT, -LIMIT, ALU.min, ALU.max))
                dve.wait_ge(gate_ready, b + 1)
                ch.link(dve.scalar_tensor_tensor(out=up_s, in0=up_s, scalar=1.0, in1=gate_s, op0=ALU.add, op1=ALU.mult))
                dve.wait_ge(sigm_ready, b + 1)
                dve.tensor_tensor(hid, up_s, sig_s, ALU.mult).then_inc(hid_ready, 1)
                make_b1_pick(nxt)
                dve.wait_ge(hidT_done, b + 1)
                dve.tensor_copy(hidT, bank[:, BH, :]).then_inc(hidT_ready, 1)
                dve.wait_ge(chunk_used, b * BLK + PRE + BLK)
                dve.wait_ge(scatter_done, b + 1)
                dve.tensor_copy(down_s, bank[:, BH, :]).then_inc(down_ready, 1)
                assert ch.n == STEPS

            expert_block(0, first=True)
            with dve.Fori(1, E) as b:
                expert_block(b)
            n_over = dve.value_load(ctrl[0:1, OVER:OVER + 1], min_val=0, max_val=OVER_MAX)
            with dve.If(n_over > 0):
                with dve.Fori(0, OVER_MAX) as j:
                    with dve.If(j < n_over):
                        expert_block(j + E)
                    dve.nop()
                dve.nop()
            dve.wait_ge(final_g_landed, 16)
            for m in range(MT):
                dve.wait_ge(ssq_act, 3 + m)
                dve.tensor_scalar(msq[:, 2, m:m + 1], ssq[:, 2, m:m + 1], 1.0 / D, EPS,
                                  ALU.mult, ALU.add).then_inc(msq_ready, 1)
                dve.wait_ge(rstd_ready, 4 + m)
                for a in range(2):
                    cols = slice(a * 512, (a + 1) * 512)
                    dve.scalar_tensor_tensor(out=h2[:, m, cols], in0=bank[:, 2 * m + a, :], scalar=rstd[:, 2, m:m + 1],
                                             in1=gf_b[:, cols], op0=ALU.mult, op1=ALU.mult).then_inc(out_ready, 1)

        @block.scalar
        def _(act):
            act.wait_ge(x_landed[1], 16)
            act.activation(h[:, 1, :], x[:, 1, :], ACT.Square, accum_out=ssq[:, 0, 1:2]).then_inc(ssq_act, 1)
            act.wait_ge(vec_ready, 1)

            def exponentials(u):
                s = prob[u % 2]
                act.wait_ge(max_ready, u + 1)
                if u >= 4:
                    act.activation(e_sink[:], e_sink[:], ACT.Exp)
                for i in range(2):
                    for qt in range(MT):
                        last = act.activation(s[:, i, qt, :], s[:, i, qt, :], ACT.Exp,
                                              bias=neg_mx[:, i, qt:qt + 1], accum_out=den[:, i, qt:qt + 1])
                last.then_inc(exp_ready, 1)

            def read_probs(u):
                act.wait_ge(probT_done, u + 1)
                if u:
                    act.wait_ge(o_done, u)
                act.activation(probT[:].rearrange("p i k t -> p (i k t)"),
                               bank[:, BT:BT + 2, :].rearrange("p b n -> p (b n)"), ACT.Identity).then_inc(probT_ready, 1)

            def read_gates(c):
                act.wait_ge(chunk_used, c + 1)
                for a in range(2):
                    b = 2 * (c - GATE_C) + a
                    last = act.activation(gates[:, b, :], half_(c % 3)[:, a, :],
                                          ACT.Identity if c < LAST_PLAIN else ACT.Sigmoid, bias=vec[:, 2 * c + a:2 * c + a + 1])
                last.then_inc(proj_read_act, 1)

            for c in range(N_IN + 1):
                turned, scored = unit_at(TURN_C, c), unit_at(UNIT_C, c)
                if turned is not None:
                    read_probs(turned)
                if c > GATE_C:
                    read_gates(c - 1)
                if scored is not None:
                    exponentials(scored)
                if c == LAST_PLAIN:
                    act.wait_ge(proj_read_act, c - GATE_C)
                    n = 2 * (c - GATE_C)
                    act.activation(gates[:, 0:n, :], gates[:, 0:n, :], ACT.Sigmoid).then_inc(sig_ready, 1)
            g2 = D_IN // P + KD
            for n in range(N_OUT):
                act.wait_ge(x2_ready, n + 1)
                for m in range(MT):
                    last = act.activation(h2[:, m, n * CW:(n + 1) * CW], x[:, m, n * CW:(n + 1) * CW], ACT.Square,
                                          accum_out=ssq_part[:, n, m:m + 1])
                if n == N_OUT - 1:
                    last.then_inc(ssq_act, 1)
                    break
                act.wait_ge(x2T_done, n + 1)
                for j in range(2):
                    k = 2 * n + j
                    last = act.activation(x2T[:, k, :], half_(4 + n % 2)[:, j, :], ACT.Identity,
                                          scale=vec[:, g2 + k:g2 + k + 1])
                last.then_inc(x2T_ready, 1)
            act.wait_ge(top_ready, 1)
            for m in range(MT):
                last = act.activation(share[:, m, 0:E], logit[:, m, :], ACT.Exp, bias=neg_top[:, m:m + 1])
            last.then_inc(top_exp, 1)

            def copy_gathered(b):
                act.wait_ge(xg_done, b + 1)
                act.activation(xg, bank[:, BX, :], ACT.Identity).then_inc(xg_ready, 1)

            def copy_gatheredT(b):
                act.wait_ge(xgT_done, b + 1)
                act.activation(xgT, bank[:, BX, :], ACT.Identity).then_inc(xgT_ready, 1)

            act.sem_inc(scatT_ready, 1)
            copy_gathered(0)
            copy_gatheredT(0)

            def place_held(i):
                s = expert_slot(BLK - 1)[0]
                act.wait_ge(chunk_used, (i + (E - HELD)) * BLK + PRE)
                act.activation(ring[:, s, :], held[:, bass.ds(i, 1), :].rearrange("p s n -> p (s n)"),
                               ACT.Identity).then_inc(landed[s], 16)

            def expert_block(b):
                act.wait_ge(gate_ready, b + 1)
                act.activation(sig_s, gate_s, ACT.Sigmoid, scale=ALPHA).then_inc(sigm_ready, 1)
                copy_gathered(b + 1)
                act.wait_ge(scatT_done, b + 2)
                act.wait_ge(scatter_done, b + 1)
                act.activation(scatT, bank[:, BU, 0:T], ACT.Identity).then_inc(scatT_ready, 1)
                copy_gatheredT(b + 1)

            expert_block(0)
            with act.Fori(1, E - HELD) as b:
                expert_block(b)
            act.wait_ge(held_landed, 16 * HELD)
            with act.Fori(0, HELD) as i:
                place_held(i)
                expert_block(i + (E - HELD))
            act.wait_ge(ctrl_ready, 1)
            n_over = act.value_load(ctrl[0:1, OVER:OVER + 1], min_val=0, max_val=OVER_MAX)
            with act.If(n_over > 0):
                with act.Fori(0, OVER_MAX) as j:
                    with act.If(j < n_over):
                        expert_block(j + E)
                    act.nop()
                act.nop()
            for m in range(MT):
                act.wait_ge(y_done, m + 1)
                act.activation(h2[:, m, :], bank[:, 2 * m:2 * m + 2, :].rearrange("p b n -> p (b n)"), ACT.Square,
                               accum_out=ssq[:, 2, m:m + 1]).then_inc(ssq_act, 1)


_INS = ["x", "norm1_g", "w_in", "b_in", "na_rpb", "swa_sinks", "w_up_a", "w_up_b", "w_out", "norm2_g",
        "w_router", "b_router", "w1", "b1", "w2", "b2", "final_g"]


def kernel(**inputs):
    import concourse.bacc as bacc
    from concourse.bass_utils import run_bass_kernel_spmd

    nc = bacc.Bacc("TRN2", target_bir_lowering=False, num_devices=1, dynamic_dma_scratch_size=1024)
    arrays, args = {}, []
    for name, a in [("consts", shape_constants())] + [(n, np.ascontiguousarray(inputs[n])) for n in _INS]:
        arrays[f"in_{name}"] = a
        args.append(nc.dram_tensor(f"in_{name}", a.shape, mybir.dt.from_np(a.dtype), kind="ExternalInput").ap())
    out = nc.dram_tensor("out_0", (1, T, D), F32, kind="ExternalOutput").ap()
    build_block(nc, *args, out)
    r = run_bass_kernel_spmd(nc, [arrays], core_ids=[0])
    return r.results[0]["out_0"]
```
